# Optimizing a Trainium2 kernel written in Bass

```python
import math
import jax, jax.numpy as jnp
from jax import lax
import numpy as np

D_MODEL = 1024
BATCH = 1
SEQ = 256
DEPTH = 4

GRID_W = 64
CTX_LEN = 256
N_MIXERS = 3
N_A = (DEPTH + 2) // 3
N_B = (DEPTH + 1) // 3
N_C = DEPTH // 3

DA_HEADS = 8
DA_HEAD_DIM = D_MODEL // (2 * DA_HEADS)
Q_BLOCK = 128

RET_HEADS = 4
RET_QK_DIM = D_MODEL // RET_HEADS
RET_V_DIM = 2 * RET_QK_DIM
RET_CHUNK = 128

NA_HEADS = 16
NA_HEAD_DIM = D_MODEL // NA_HEADS
NA_KH = 8
NA_KW = 16

FFN_HIDDEN = -(-8 * D_MODEL // (3 * 256)) * 256
ROPE_BASE = 10000.0
EPS = 1e-6
F32 = jnp.float32

kernel_name = 'hybrid_diffattn_retention_natten_prefix_trunk'

def _rms(x):
    x32 = x.astype(F32)
    return x32 * lax.rsqrt(jnp.mean(x32 * x32, axis=-1, keepdims=True) + EPS)

def rms_norm(x, g):
    return (_rms(x) * g.astype(F32)).astype(x.dtype)

def modulate(x, g, shift, scale):
    return rms_norm(x, g) * (1 + scale) + shift

def ada_mod(cond, w, b):
    m = jax.nn.silu(cond) @ w + b
    return [a[:, None, :] for a in jnp.split(m, 6, axis=-1)]

def axial_rope(x, rows, cols):
    d = x.shape[-1]
    f = d // 4
    inv = ROPE_BASE ** (-jnp.arange(f, dtype=F32) / f)
    ang = jnp.concatenate([rows.astype(F32)[:, None] * inv, cols.astype(F32)[:, None] * inv], axis=-1)[:, None, :]
    cos, sin = jnp.cos(ang), jnp.sin(ang)
    x32 = x.astype(F32)
    x1, x2 = x32[..., : d // 2], x32[..., d // 2:]
    return jnp.concatenate([x1 * cos - x2 * sin, x1 * sin + x2 * cos], axis=-1).astype(x.dtype)

def swiglu(h, w_in, w_out):
    a, b = jnp.split(h @ w_in, 2, axis=-1)
    return (jax.nn.silu(a) * b) @ w_out

def _diff_core(q, k, v, lam, scale):
    s = jnp.einsum('bqnd,bknd->bnqk', q, k).astype(F32) * scale
    p = jax.nn.softmax(s, axis=-1)
    b, n, tq, tk = p.shape
    p = p.reshape(b, n // 2, 2, tq, tk)
    a = p[:, :, 0] - lam * p[:, :, 1]
    return jnp.einsum('bhqk,bkhe->bqhe', a.astype(v.dtype), v)

def diff_attention(hx, hz, w_qkv, w_o, lam_p, subln_g, lam_init, rows, cols, need_ctx):
    B, L, D = hx.shape
    H, dh = DA_HEADS, DA_HEAD_DIM

    def qkv(h):
        T = h.shape[1]
        q, k, v = jnp.split(h @ w_qkv, 3, axis=-1)
        return q.reshape(B, T, 2 * H, dh), k.reshape(B, T, 2 * H, dh), v.reshape(B, T, H, 2 * dh)

    qx, kx, vx = qkv(hx)
    qz, kz, vz = qkv(hz)
    qx = axial_rope(qx, rows, cols)
    kx = axial_rope(kx, rows, cols)
    lp = lam_p.astype(F32)
    lam = jnp.exp(jnp.sum(lp[0] * lp[1])) - jnp.exp(jnp.sum(lp[2] * lp[3])) + lam_init
    scale = dh ** -0.5
    k_all = jnp.concatenate([kx, kz], axis=1)
    v_all = jnp.concatenate([vx, vz], axis=1)
    nb = L // Q_BLOCK
    qb = jnp.moveaxis(qx.reshape(B, nb, Q_BLOCK, 2 * H, dh), 1, 0)
    ox = lax.map(lambda qi: _diff_core(qi, k_all, v_all, lam, scale), qb)
    ox = jnp.moveaxis(ox, 0, 1).reshape(B, L, H, 2 * dh)

    def finish(o):
        o = rms_norm(o, subln_g) * (1.0 - lam_init)
        return o.reshape(B, o.shape[1], H * 2 * dh) @ w_o

    out_x = finish(ox)
    out_z = finish(_diff_core(qz, kz, vz, lam, scale)) if need_ctx else None
    return out_x, out_z

def _retention_scan(q, k, v, log_g, S0, inclusive):
    B, T, H, dk = q.shape
    dv = v.shape[-1]
    C = RET_CHUNK
    n = T // C

    def chunks(a):
        return jnp.moveaxis(a.astype(F32).reshape(B, n, C, H, a.shape[-1]), 1, 0)

    idx = jnp.arange(C, dtype=F32)
    diff = idx[:, None] - idx[None, :]
    mask = (diff >= 0) if inclusive else (diff > 0)
    dmat = jnp.where(mask[None], jnp.exp(jnp.maximum(diff, 0.0)[None] * log_g[:, None, None]), 0.0)
    xi = jnp.exp((idx[:, None] + 1.0) * log_g[None, :])
    zeta = jnp.exp((C - 1.0 - idx)[:, None] * log_g[None, :])
    decay_c = jnp.exp(C * log_g)

    def step(S, inp):
        qc, kc, vc = inp
        s = jnp.einsum('bihd,bjhd->bhij', qc, kc) * dmat
        o = jnp.einsum('bhij,bjhe->bihe', s, vc) + jnp.einsum('bihd,bhde->bihe', qc, S) * xi[None, :, :, None]
        S = S * decay_c[None, :, None, None] + jnp.einsum('bjhd,bjhe->bhde', kc * zeta[None, :, :, None], vc)
        return S, o

    S, o = lax.scan(step, S0, (chunks(q), chunks(k), chunks(v)))
    return jnp.moveaxis(o, 0, 1).reshape(B, T, H, dv), S

def retention(hx, hz, w_in, w_o, decay_logit, rows, cols, need_ctx):
    B = hx.shape[0]
    H, dk, dv = RET_HEADS, RET_QK_DIM, RET_V_DIM

    def proj(h):
        T = h.shape[1]
        q, k, v, g = jnp.split(h @ w_in, [H * dk, 2 * H * dk, 2 * H * dk + H * dv], axis=-1)
        return q.reshape(B, T, H, dk), k.reshape(B, T, H, dk) * dk ** -0.5, v.reshape(B, T, H, dv), g

    qx, kx, vx, gx = proj(hx)
    qz, kz, vz, gz = proj(hz)
    qx = axial_rope(qx, rows, cols)
    kx = axial_rope(kx, rows, cols)
    log_g = jax.nn.log_sigmoid(decay_logit.astype(F32))
    S0 = jnp.zeros((B, H, dk, dv), F32)

    def flip(a):
        return a[:, ::-1]

    oz_f, Sz_f = _retention_scan(qz, kz, vz, log_g[0], S0, True)
    ox_f, _ = _retention_scan(qx, kx, vx, log_g[0], Sz_f, True)
    oz_b, Sz_b = _retention_scan(flip(qz), flip(kz), flip(vz), log_g[1], S0, False)
    ox_b, _ = _retention_scan(flip(qx), flip(kx), flip(vx), log_g[1], Sz_b, False)

    def finish(o, g):
        T = o.shape[1]
        o = _rms(o).reshape(B, T, H * dv).astype(g.dtype)
        return (jax.nn.silu(g) * o) @ w_o

    out_x = finish(ox_f + flip(ox_b), gx)
    out_z = finish(oz_f + flip(oz_b), gz) if need_ctx else None
    return out_x, out_z

def neighborhood_attention(hx, hz, w_qkv, w_o, rpb, need_ctx):
    B, L, D = hx.shape
    H, dh = NA_HEADS, NA_HEAD_DIM
    R = L // GRID_W
    W = GRID_W
    kh = min(NA_KH, R)
    kw = NA_KW
    scale = dh ** -0.5

    def qkv(h):
        T = h.shape[1]
        q, k, v = jnp.split(h @ w_qkv, 3, axis=-1)
        return q.reshape(B, T, H, dh), k.reshape(B, T, H, dh), v.reshape(B, T, H, dh)

    qx, kx, vx = qkv(hx)
    qz, kz, vz = qkv(hz)
    kg = kx.reshape(B, R, W, H, dh)
    vg = vx.reshape(B, R, W, H, dh)
    col = jnp.arange(W)
    cs = jnp.clip(col - kw // 2, 0, W - kw)
    col_ok = (col[None, :] >= cs[:, None]) & (col[None, :] < cs[:, None] + kw)
    dc_idx = jnp.clip(col[None, :] - col[:, None] + NA_KW - 1, 0, 2 * NA_KW - 2)
    rpb32 = rpb.astype(F32)

    def row_block(args):
        r, qr = args
        rs = jnp.clip(r - kh // 2, 0, R - kh)
        kb = lax.dynamic_slice_in_dim(kg, rs, kh, axis=1)
        vb = lax.dynamic_slice_in_dim(vg, rs, kh, axis=1)
        dr_idx = rs + jnp.arange(kh) - r + NA_KH - 1
        bias = rpb32[:, dr_idx[:, None, None], dc_idx[None, :, :]]
        bias = jnp.where(col_ok[None, None], bias, -jnp.inf).transpose(0, 2, 1, 3)
        s_lat = jnp.einsum('bqhd,bkwhd->bhqkw', qr, kb).astype(F32) * scale + bias
        s_ctx = jnp.einsum('bqhd,bnhd->bhqn', qr, kz).astype(F32) * scale
        s = jnp.concatenate([s_lat.reshape(B, H, W, kh * W), s_ctx], axis=-1)
        p = jax.nn.softmax(s, axis=-1).astype(vb.dtype)
        p_lat = p[..., : kh * W].reshape(B, H, W, kh, W)
        return (jnp.einsum('bhqkw,bkwhd->bqhd', p_lat, vb)
                + jnp.einsum('bhqn,bnhd->bqhd', p[..., kh * W:], vz))

    qg = jnp.moveaxis(qx.reshape(B, R, W, H, dh), 1, 0)
    ox = lax.map(row_block, (jnp.arange(R), qg))
    out_x = jnp.moveaxis(ox, 0, 1).reshape(B, L, D) @ w_o
    out_z = None
    if need_ctx:
        s = jnp.einsum('bqhd,bkhd->bhqk', qz, kz).astype(F32) * scale
        p = jax.nn.softmax(s, axis=-1).astype(vz.dtype)
        oz = jnp.einsum('bhqk,bkhd->bqhd', p, vz)
        out_z = oz.reshape(B, oz.shape[1], D) @ w_o
    return out_x, out_z

def setup_inputs(seed: int = 0) -> dict:
    key = jax.random.key(seed)
    ks = jax.random.split(key, 24)
    D = D_MODEL

    def nrm(k, shape, s):
        return jax.random.normal(k, shape, F32) * s

    gamma0 = 1.0 - 2.0 ** (-5.0 - jnp.arange(RET_HEADS, dtype=F32))
    decay_base = jnp.log(gamma0) - jnp.log1p(-gamma0)
    ret_in_w = 2 * RET_HEADS * RET_QK_DIM + 2 * RET_HEADS * RET_V_DIM
    return {
        'x': nrm(ks[0], (BATCH, SEQ, D), 1.0),
        'c': nrm(ks[1], (BATCH, D), 1.0),
        'ctx': nrm(ks[2], (BATCH, CTX_LEN, D), 1.0),
        'c_ctx': nrm(ks[3], (D,), 1.0),
        'w_ada': nrm(ks[4], (DEPTH, D, 6 * D), 0.5 * D ** -0.5),
        'b_ada': nrm(ks[5], (DEPTH, 6 * D), 0.02),
        'norm_g': 1.0 + nrm(ks[6], (DEPTH, 2, D), 0.02),
        'ffn_in': nrm(ks[7], (DEPTH, D, 2 * FFN_HIDDEN), D ** -0.5),
        'ffn_out': nrm(ks[8], (DEPTH, FFN_HIDDEN, D), FFN_HIDDEN ** -0.5),
        'final_g': 1.0 + nrm(ks[9], (D,), 0.02),
        'da_w_qkv': nrm(ks[10], (N_A, D, 3 * D), D ** -0.5),
        'da_w_o': nrm(ks[11], (N_A, D, D), D ** -0.5),
        'da_lambda': nrm(ks[12], (N_A, 4, DA_HEAD_DIM), 0.1),
        'da_subln': 1.0 + nrm(ks[13], (N_A, 2 * DA_HEAD_DIM), 0.02),
        'ret_w_in': nrm(ks[14], (N_B, D, ret_in_w), D ** -0.5),
        'ret_w_o': nrm(ks[15], (N_B, RET_HEADS * RET_V_DIM, D), (RET_HEADS * RET_V_DIM) ** -0.5),
        'ret_decay': decay_base[None, None, :] + nrm(ks[16], (N_B, 2, RET_HEADS), 0.1),
        'na_w_qkv': nrm(ks[17], (N_C, D, 3 * D), D ** -0.5),
        'na_w_o': nrm(ks[18], (N_C, D, D), D ** -0.5),
        'na_rpb': nrm(ks[19], (N_C, NA_HEADS, 2 * NA_KH - 1, 2 * NA_KW - 1), 0.02),
    }

def reference(x, c, ctx, c_ctx, w_ada, b_ada, norm_g, ffn_in, ffn_out, final_g,
              da_w_qkv, da_w_o, da_lambda, da_subln,
              ret_w_in, ret_w_o, ret_decay,
              na_w_qkv, na_w_o, na_rpb):
    B, L, D = x.shape
    t = jnp.arange(L)
    rows = t // GRID_W
    cols = t % GRID_W
    z = ctx
    cz = c_ctx[None, :]
    ia = ib = ic = 0
    for li in range(DEPTH):
        kind = li % N_MIXERS
        need_ctx = li < DEPTH - 1
        sh1, sc1, gt1, sh2, sc2, gt2 = ada_mod(c, w_ada[li], b_ada[li])
        zsh1, zsc1, zgt1, zsh2, zsc2, zgt2 = ada_mod(cz, w_ada[li], b_ada[li])
        hx = modulate(x, norm_g[li, 0], sh1, sc1)
        hz = modulate(z, norm_g[li, 0], zsh1, zsc1)
        if kind == 0:
            lam_init = 0.8 - 0.6 * math.exp(-0.3 * li)
            ox, oz = diff_attention(hx, hz, da_w_qkv[ia], da_w_o[ia], da_lambda[ia], da_subln[ia],
                                    lam_init, rows, cols, need_ctx)
            ia += 1
        elif kind == 1:
            ox, oz = retention(hx, hz, ret_w_in[ib], ret_w_o[ib], ret_decay[ib], rows, cols, need_ctx)
            ib += 1
        else:
            ox, oz = neighborhood_attention(hx, hz, na_w_qkv[ic], na_w_o[ic], na_rpb[ic], need_ctx)
            ic += 1
        x = x + gt1 * ox
        x = x + gt2 * swiglu(modulate(x, norm_g[li, 1], sh2, sc2), ffn_in[li], ffn_out[li])
        if need_ctx:
            z = z + zgt1 * oz
            z = z + zgt2 * swiglu(modulate(z, norm_g[li, 1], zsh2, zsc2), ffn_in[li], ffn_out[li])
    return rms_norm(x, final_g)


_drawn_inputs = setup_inputs


def setup_inputs(seed=0):
    import zlib

    import numpy as np

    out = dict(_drawn_inputs(seed))
    spreads = {}
    factors = {'norm_g': 3.697, 'final_g': 7.923, 'da_lambda': 4.369, 'da_subln': 7.722, 'na_rpb': 64.0}
    for name, (base, spread) in spreads.items():
        noise = np.random.default_rng([zlib.crc32(name.encode()), seed]).standard_normal(out[name].shape)
        drawn = base * np.exp(spread * noise) if base else spread * noise
        out[name] = __import__('jax').numpy.asarray(drawn.astype(out[name].dtype))
    for name, factor in factors.items():
        out[name] = (out[name] * factor).astype(out[name].dtype)
    return out
```

```python
import math
from contextlib import ExitStack

import numpy as np

import concourse.bass as bass
from concourse import mybir

F32 = mybir.dt.float32
F32R = mybir.dt.float32r
F16 = mybir.dt.float16
ALU = mybir.AluOpType
ACT = mybir.ActivationFunctionType
AX = mybir.AxisListType

P = 128
D = 1024
KT = D // P
SEQ = 256
CTX = 256
TOK = SEQ + CTX
DEPTH = 4
GRID_W = 64
ROWS = SEQ // GRID_W
HIDDEN = -(-8 * D // (3 * 256)) * 256
JT = HIDDEN // P
DA_HEADS = 8
DA_DIM = D // (2 * DA_HEADS)
RET_HEADS = 4
RET_QK = D // RET_HEADS
RET_V = 2 * RET_QK
ET = RET_V // P
NA_HEADS = 16
NA_KH, NA_KW = 8, 16
NA_DIM = D // NA_HEADS
RPB_W = 2 * NA_KW - 1
RPB_PAD = 2 * GRID_W - 1
MOD = 6 * KT
EPS = 1e-6
RING = 4
AHEAD = 2
ADA_RING = 2
KINDS = [li % 3 for li in range(DEPTH)]
MIXER_UNITS = {0: 4 * KT, 1: RET_HEADS * 12 + 2 * KT, 2: 4 * KT}
FFN_UNITS = 3 * JT
UNITS = sum(MIXER_UNITS[k] + FFN_UNITS for k in KINDS)


def shape_tables():
    t = np.arange(SEQ)
    rows, cols = (t // GRID_W).astype(np.float32), (t % GRID_W).astype(np.float32)

    def angles(f):
        inv = (np.float32(10000.0) ** (-np.arange(f, dtype=np.float32) / np.float32(f))).astype(np.float32)
        return np.concatenate([inv[:, None] * rows, inv[:, None] * cols], 0).astype(np.float32)

    a = angles(DA_DIM // 4)
    half = DA_DIM // 2
    ang = np.stack([a[p % half] for p in range(P)])
    sign = np.array([1.0 if p % DA_DIM < half else -1.0 for p in range(P)], np.float32)[:, None]
    c, s = np.cos(ang), np.sin(ang) * sign
    q = np.float32(DA_DIM ** -0.5)
    da_rope = np.stack([c * q, s * q, c, s], 1).astype(np.float32)
    b = angles(RET_QK // 4)
    ret_rope = np.stack([np.cos(b), np.sin(b)], 1).astype(np.float32)
    key = (np.arange(2)[None, :, None] * P + np.arange(P)[:, None, None])
    qry = np.arange(SEQ)[None, None, :]
    ret_exp = np.stack([np.maximum(qry - key, 0), np.maximum(key - qry, 0),
                        CTX + qry - key, CTX - qry + key], 1).astype(np.float16)
    col = np.arange(GRID_W)
    cs = np.clip(col - NA_KW // 2, 0, GRID_W - NA_KW)
    ok = (col[None, :] >= cs[:, None]) & (col[None, :] < cs[:, None] + NA_KW)
    mask = np.where(ok, 0.0, -3.0e38).astype(np.float32)
    return {"da_rope": da_rope, "ret_rope": ret_rope, "ret_exp": ret_exp,
            "na_mask": np.concatenate([mask, mask], 0), "ident": np.eye(P, dtype=np.float32)}


class Links:

    def __init__(self, eng, sem):
        self.eng, self.sem, self.base, self.n = eng, sem, 0, 0

    def __call__(self, ins):
        self.n += 1
        ins.then_inc(self.sem, 1)
        self.eng.wait_ge(self.sem, self.base + self.n)

    def loop(self, trips, per):
        return _LinkedLoop(self, trips, per)


class _LinkedLoop:
    def __init__(self, links, trips, per):
        self.links, self.trips, self.per = links, trips, per
        self.start = links.n
        self.loop = links.eng.Fori(0, trips)

    def __enter__(self):
        i = self.loop.__enter__()
        self.links.base, self.links.n = i * self.per + self.start, 0
        return i

    def __exit__(self, *error):
        if error[0] is None:
            assert self.links.n == self.per, self.links.n
        self.links.base, self.links.n = 0, self.start + self.trips * self.per
        return self.loop.__exit__(*error)


class Layer:

    def __init__(self, sem, li, first_unit):
        self.li, self.kind, self.par = li, KINDS[li], li % 2
        self.n, self.nf = first_unit, first_unit + MIXER_UNITS[self.kind]
        self.zq = li < DEPTH - 1
        self.W = TOK if self.zq else SEQ
        self.na = self.kind == 2
        self.da = sum(k == 0 for k in KINDS[:li])
        self.banks = 6 if self.zq else 4
        self.groups = (3 if self.zq else 2) * (2 if self.na else 1)
        self.v_done = sem(f"v_done_{li}")
        self.v_act = sem(f"v_act_{li}")
        self.v_dve = sem(f"v_dve_{li}")
        self.s_done = sem(f"s_done_{li}")
        self.osq_ready = sem(f"osq_ready_{li}")
        self.oms_done = sem(f"oms_done_{li}")
        self.ors_ready = sem(f"ors_ready_{li}")
        self.y_ready = sem(f"y_ready_{li}")
        self.y_hi_ready = sem(f"y_hi_ready_{li}")
        self.y_lo_ready = sem(f"y_lo_ready_{li}")
        if self.kind == 1:
            self.darg_ready = sem(f"darg_ready_{li}")
            self.dexp_ready = sem(f"dexp_ready_{li}")
            self.rot_ready = sem(f"rot_ready_{li}")
            self.zcopy_ready = sem(f"zcopy_ready_{li}")
            self.sT_ready = sem(f"sT_ready_{li}")
            self.o_done = sem(f"o_done_{li}")
            self.silu_g = sem(f"silu_g_{li}")
        else:
            self.qk_dve = sem(f"qk_dve_{li}")
            self.qk_act = sem(f"qk_act_{li}")
            self.negmax = sem(f"negmax_{li}")
            self.e_ready = sem(f"e_ready_{li}")
            self.a_ready = sem(f"a_ready_{li}")
            self.t_done = sem(f"t_done_{li}")
            self.aT_ready = sem(f"aT_ready_{li}")
            self.vst_ready = sem(f"vst_ready_{li}")
            self.pv_done = sem(f"pv_done_{li}")
        self.silu_ready = sem(f"silu_ready_{li}")
        self.u_free = sem(f"u_free_{li}")
        self.u_hi_ready = sem(f"u_hi_ready_{li}")
        self.u_lo_ready = sem(f"u_lo_ready_{li}")
        self.out_done = sem(f"out_done_{li}")


def trunk(nc, xT_in, cond_in, weights, ada_w, ada_b, gains, final_g, lam_in, subln_in, decay_in,
          rpb_in, da_rope_in, ret_rope_in, ret_exp_in, na_mask_in, ident_in, out, layers=DEPTH):
    with ExitStack() as ctx:
        def sb(name, shape, dt=F32, at=ctx):
            return at.enter_context(nc.sbuf_tensor(name, shape, dt))

        def sem(name):
            return ctx.enter_context(nc.semaphore(name))

        w_raw = sb("w_raw", [P, RING, D])
        w_hi = sb("w_hi", [P, RING, D], F32R)
        w_lo = sb("w_lo", [P, RING, D], F32R)
        xT = sb("xT", [P, KT, TOK])
        h_hi = sb("h_hi", [P, KT, TOK], F32R)
        h_lo = sb("h_lo", [P, KT, TOK], F32R)
        mod = sb("mod", [P, 2, MOD, 2])
        amp = sb("amp", [P, 2, 2, KT, 2])
        cond = sb("cond", [P, KT, 2])
        cond_raw = sb("cond_raw", [P, KT, 2])
        bias_ada = sb("bias_ada", [P, DEPTH, MOD])
        gain = sb("gain", [P, DEPTH, 2, KT])
        gain_f = sb("gain_f", [P, KT])
        eps_c = sb("eps_c", [P, 1])
        one_c = sb("one_c", [P, 1])
        ones = sb("ones", [P, P])
        ident = sb("ident", [P, P])
        ssum = sb("ssum", [P, TOK])
        lnm = sb("lnm", [P, TOK])
        rstd = sb("rstd", [P, TOK])
        tmp = sb("tmp", [P, 2, TOK])
        lam_sb = rstd[:, :].rearrange("p (l a d) -> p l a d", l=2, a=4)
        lam_pr = lnm[:, 0:4 * DA_DIM].rearrange("p (l a d) -> p l a d", l=2, a=2)
        lam_sum = sb("lam_sum", [P, 2, 2])
        neg_lam = sb("neg_lam", [P, 2])
        subln = sb("subln", [P, 2])
        logit = sb("logit", [P, 2 * RET_HEADS])
        lg_t = sb("lg_t", [P, 4, 2 * RET_HEADS])
        log_g = sb("log_g", [P, 2, RET_HEADS])
        lg_cur = sb("lg_cur", [P, 2])

        with ExitStack() as s:
            u_hi = sb("u_hi", [P, JT, TOK], F32R, s)
            u_lo = sb("u_lo", [P, JT, TOK], F32R, s)
            ada_raw = sb("ada_raw", [P, ADA_RING, D], F32, s)
        with ExitStack() as s:
            y_hi = sb("y_hi", [P, KT, TOK], F32R, s)
            y_lo = sb("y_lo", [P, KT, TOK], F32R, s)
            v_all = sb("v_all", [P, 4, D], F32, s)
            v_st = sb("v_st", [P, 4, P], F32, s)
            qT = sb("qT", [P, TOK], F32, s)
            kT = sb("kT", [P, TOK], F32, s)
            with ExitStack() as s2:
                da_rope = sb("da_rope", [P, 4, SEQ], F32, s2)
                qk_raw = sb("qk_raw", [P, 2, SEQ], F32, s2)
                rot = sb("rot", [P, 2, SEQ], F32, s2)
                e_x = sb("e_x", [P, 2, 2, TOK], F32, s2)
                e_z = sb("e_z", [P, 2, 2, CTX], F32, s2)
                a_x = sb("a_x", [P, 2, TOK], F32, s2)
                a_z = sb("a_z", [P, 2, CTX], F32, s2)
                aT = sb("aT", [P, 3, TOK], F32, s2)
                d_st = sb("d_st", [P, 4, 8], F32, s2)
            with ExitStack() as s2:
                rpb_rows = sb("rpb_rows", [NA_HEADS * 7, RPB_PAD], F32, s2)
                na_mask = sb("na_mask", [P, GRID_W], F32, s2)
                bias = sb("bias", [P, 2, 2, 2, SEQ], F32, s2)
                n_x = sb("n_x", [P, 2, 2, TOK], F32, s2)
                n_z = sb("n_z", [P, 2, 2, CTX], F32, s2)
                nT = sb("nT", [P, 2, 3, TOK], F32, s2)
                n_st = sb("n_st", [P, 3, 8], F32, s2)
        with ExitStack() as s:
            ry_hi = sb("ry_hi", [P, RET_HEADS * ET, TOK], F32R, s)
            ry_lo = sb("ry_lo", [P, RET_HEADS * ET, TOK], F32R, s)
            rv = sb("rv", [P, 4, RET_V], F32, s)
            rq = sb("rq", [P, 4, TOK], F32, s)
            ret_rope = sb("ret_rope", [P, 2, SEQ], F32, s)
            ret_exp = sb("ret_exp", [P, 4, 2, SEQ], F16, s)
            decay = sb("decay", [P, 2, 2, SEQ], F32, s)
            darg = sb("darg", [P, 2, SEQ], F32, s)
            sT = sb("sT", [P, 3, TOK], F32, s)
        rpb_skew = nc.dram_tensor("rpb_skew", (NA_HEADS * 7, GRID_W, RPB_PAD), F32, kind="Internal").ap()

        bank = [ctx.enter_context(nc.psum_tensor(f"bank{b}", [P, TOK], F32)) for b in range(8)]

        raw_loaded = [sem(f"raw_loaded{r}") for r in range(RING)]
        small_in, table_in = sem("small_in"), sem("table_in")
        hi_ready, lo_ready, unit_used = sem("hi_ready"), sem("lo_ready"), sem("unit_used")
        ada_loaded = [sem(f"ada_loaded{r}") for r in range(ADA_RING)]
        ada_done, mod_ready, cond_ready, consts = sem("ada_done"), sem("mod_ready"), sem("cond_ready"), sem("consts")
        dve_own, act_own = sem("dve_own"), sem("act_own")
        lam_sums, lam_exps, log_abs, log_parts = sem("lam_sums"), sem("lam_exps"), sem("log_abs"), sem("log_parts")
        x_new, sq_ready, ssum_step = sem("x_new"), sem("sq_ready"), sem("ssum_step")
        ms_done, rstd_ready = sem("ms_done"), sem("rstd_ready")
        norm_t, h_hi_ready, h_ready = sem("norm_t"), sem("h_hi_ready"), sem("h_ready")
        fin_ready, stored = sem("fin_ready"), sem("stored")
        skew_in, skew_out, rpb_zero = sem("skew_in"), sem("skew_out"), sem("rpb_zero")
        bias_in = [sem("bias_in0"), sem("bias_in1")]

        plan = []
        first_unit = 0
        for li in range(layers):
            plan.append(Layer(sem, li, first_unit))
            first_unit += MIXER_UNITS[KINDS[li]] + FFN_UNITS
        UN = first_unit
        SMALL = 16 * 9
        NORMS = 2 * layers

        block = ctx.enter_context(nc.Block())

        def gate_buf(e):
            return lnm[:, :] if e % 2 == 0 else darg[:, :, :].rearrange("p a n -> p (a n)")

        @block.sync
        def _(sp):
            sp.dma_start(cond_raw[:, :, :], cond_in).then_inc(small_in, 16)
            sp.dma_start(xT[:, :, :], xT_in).then_inc(small_in, 16)
            for dst, src in ((bias_ada, ada_b), (gain, gains), (gain_f, final_g), (subln, subln_in),
                             (ident, ident_in)):
                sp.dma_start(dst[tuple([slice(None)] * len(dst.shape))], src).then_inc(small_in, 16)
            sp.dma_start(lam_sb[:, :, :, :], lam_in.partition_broadcast(P)).then_inc(small_in, 16)
            sp.dma_start(logit[:, :], decay_in.partition_broadcast(P)).then_inc(small_in, 16)
            for r in range(RING):
                sp.dma_start(w_raw[:, r, :], weights[r]).then_inc(raw_loaded[r], 16)
            with sp.Fori(0, UN // RING - 1) as i:
                for r in range(RING):
                    sp.wait_ge(lo_ready, i * RING + r + 1)
                    sp.dma_start(w_raw[:, r, :], weights[bass.ds(i * RING + RING + r, 1)]
                                 .rearrange("a p n -> (a p) n")).then_inc(raw_loaded[r], 16)
            sp.wait_ge(fin_ready, KT)
            sp.dma_start(out, xT[:, :, 0:SEQ if layers == DEPTH else TOK]).then_inc(stored, 16)
            sp.wait_ge(stored, 16)

        @block.gpsimd
        def _(pool):
            nc.gpsimd.memset(ones[:, :], 1.0).then_inc(consts, 1)
            nc.gpsimd.memset(eps_c[:, :], EPS).then_inc(consts, 1)
            nc.gpsimd.memset(one_c[:, :], 1.0).then_inc(consts, 1)
            with pool.Fori(0, UN // RING) as i:
                for r in range(RING):
                    pool.wait_ge(hi_ready, i * RING + r + 1)
                    nc.gpsimd.tensor_tensor(out=w_lo[:, r, :], in0=w_raw[:, r, :], in1=w_hi[:, r, :],
                                            op=ALU.subtract).then_inc(lo_ready, 1)

        @block.tensor
        def _(pe):
            def mm(dst, lhsT, rhs, start, stop, **kw):
                return nc.tensor.matmul(dst, lhsT, rhs, start=start, stop=stop, **kw)

            def three(dst, stat, mov, start, stop, **kw):
                mm(dst, stat[0], mov[0], start, False, **kw)
                mm(dst, stat[0], mov[1], False, False, **kw)
                return mm(dst, stat[1], mov[0], False, stop, **kw)

            def weight(slot, a, b):
                r = slot % RING
                return w_hi[:, r, a:b], w_lo[:, r, a:b]

            def take(n):
                pe.wait_ge(lo_ready, n + 1)

            def unit(n, slot, dst, src, W, k0=0, start=True, stop=True, first_of=None):
                take(n)
                for k in range(KT):
                    if first_of is not None:
                        pe.wait_ge(h_ready, first_of * KT + k + 1)
                    last = three(dst[:, 0:W], weight(slot, k * P, k * P + P),
                                 (src[0][:, k0 + k, 0:W], src[1][:, k0 + k, 0:W]),
                                 start and k == 0, stop and k == KT - 1)
                return last

            H = (h_hi, h_lo)

            def ada_step(la, a, slot):
                pe.wait_ge(ada_loaded[slot], a * (16 // ADA_RING) + 16 * (la * (MOD // ADA_RING) + 1)
                           - slot * (16 // ADA_RING))
                for k in range(KT):
                    last = mm(bank[6][:, bass.ds(a * 2, 2)], ada_raw[:, slot, k * P:k * P + P],
                              cond[:, k, :], k == 0, k == KT - 1)
                last.then_inc(ada_done, 1)

            def norm(q, W):
                pe.wait_ge(ssum_step, KT * (q + 1))
                mm(bank[7][:, 0:W], ones[:, :], ssum[:, 0:W], True, True).then_inc(ms_done, 1)

            def values(L, q):
                with pe.Fori(0, 2) as i:
                    for s in range(4):
                        take(i * 4 + (L.n + s))
                        for kk in range(2):
                            k = 2 * s + kk
                            pe.wait_ge(h_ready, q * KT + k + 1)
                            for tb in range(4):
                                last = three(bank[tb][:, :], tuple(t[:, k, tb * P:tb * P + P] for t in H),
                                             weight(L.n + s, kk * 512, kk * 512 + 512), k == 0, k == KT - 1)
                                if k == KT - 1 and tb < 3:
                                    last.then_inc(L.v_done, 1)
                        last.then_inc(unit_used, 1)
                    pe.wait_ge(L.v_act, i * 2 + 2)
                    pe.wait_ge(L.v_dve, i * 2 + 2)

            def attention(L):
                n = L.n + KT
                subs = 2 if L.na else 1
                per = L.groups // subs

                def transposes(t, sub):
                    for g in range(per):
                        if sub == 1:
                            pe.wait_ge(L.aT_ready, t * L.groups + (g + 1))
                        for c in range(4):
                            kb, qb = (c // 2, c % 2) if g == 0 else (g + 1, c) if L.zq else (2 + c // 2, c % 2)
                            src = n_x[:, qb % 2, sub, :] if L.na else a_x[:, qb % 2, :]
                            if qb >= 2:
                                src = n_z[:, sub, qb - 2, :] if L.na else a_z[:, qb - 2, :]
                                kb -= 2
                            last = nc.tensor.transpose(bank[g][:, c * P:c * P + P], src[:, kb * P:kb * P + P],
                                                       ident[:, :])
                        last.then_inc(L.t_done, 1)

                def values_product(t, sub):
                    pe.wait_ge(L.aT_ready, t * L.groups + per * (sub + 1))
                    lo, hi = (64 * sub, 64 * sub + 64) if L.na else (0, P)
                    for j, kb in enumerate((2, 3, 0, 1)):
                        if kb >= 2 and L.zq:
                            g, a, w = kb - 1, 0, TOK
                        else:
                            g, a, w = kb // 2, (kb % 2) * SEQ, SEQ
                        mov = (nT[:, sub, g, a:a + w] if L.na else aT[:, g, a:a + w])
                        last = mm(bank[6][lo:hi, 0:w], v_st[:, kb, lo:hi], mov, j == 0, j == 3)
                    return last

                def back(t):
                    pe.wait_ge(L.a_ready, t + 1)
                    for sub in range(subs):
                        transposes(t, sub)
                    pe.wait_ge(L.vst_ready, t + 1)
                    for sub in range(subs):
                        last = values_product(t, sub)
                    last.then_inc(L.pv_done, 1)

                def mean_square(t):
                    pe.wait_ge(L.osq_ready, t + 1)
                    mm(bank[7][:, 0:L.W], ones[:, :], tmp[:, 1, 0:L.W], True, True).then_inc(L.oms_done, 1)

                def score(j):
                    lo, hi = 64 * (j % 2), 64 * (j % 2) + 64
                    if j < 4:
                        qb = j // 2
                        last = mm(bank[j][:, :], qT[lo:hi, qb * P:qb * P + P], kT[lo:hi, :], True, True)
                    else:
                        for qb in range(2):
                            last = mm(bank[j][:, qb * CTX:qb * CTX + CTX],
                                      qT[lo:hi, SEQ + qb * P:SEQ + qb * P + P], kT[lo:hi, SEQ:TOK], True, True)
                    last.then_inc(L.s_done, 1)

                def tile(t, slot, place):
                    if place >= 2:
                        pe.wait_ge(L.y_lo_ready if L.na else L.y_ready, t - 1)
                    unit(t * 2 + n, slot, bank[6], H, L.W).then_inc(unit_used, 1)
                    unit(t * 2 + (n + 1), slot + 1, bank[7], H, TOK).then_inc(unit_used, 1)
                    if place >= 1:
                        pe.wait_ge(L.qk_act, t * (1 if L.na else 2) + 1)
                        back(t - 1)
                    dv, ac = (1, 1) if L.na else (2, 2)
                    pe.wait_ge(L.qk_dve, t * dv + dv)
                    pe.wait_ge(L.qk_act, t * ac + ac)
                    for j in range(L.banks):
                        score(j)
                        if j == 1 and place >= 1 and not L.na:
                            mean_square(t - 1)

                tile(0, n, 0)
                tile(1, n + 2, 1)
                with pe.Fori(0, (KT - 2) // 2) as i:
                    for s in range(2):
                        tile(i * 2 + (2 + s), n + 2 * s, 2)
                pe.wait_ge(L.y_lo_ready if L.na else L.y_ready, KT - 1)
                back(KT - 1)
                if not L.na:
                    mean_square(KT - 1)

            def project(L, e0):
                if L.kind != 1:
                    n = L.n + 3 * KT
                    pe.wait_ge(L.y_lo_ready, KT)
                    with pe.Fori(0, 2) as i:
                        for s in range(4):
                            pe.wait_ge(x_new, i * 4 + (e0 + s - 3))
                            unit(i * 4 + (n + s), n + s, bank[s], (y_hi, y_lo), L.W).then_inc(unit_used, 1)
                else:
                    n = L.n + 12 * RET_HEADS
                    pe.wait_ge(L.y_lo_ready, RET_HEADS * ET)
                    with pe.Fori(0, 4) as i:
                        for s in range(2):
                            pe.wait_ge(x_new, i * 2 + (e0 + s - 1))
                            for part in range(2):
                                u = 2 * s + part
                                unit(i * 4 + (n + u), n + u, bank[s], (ry_hi, ry_lo), L.W, KT * part,
                                     part == 0, part == 1).then_inc(unit_used, 1)

            def retention(L, q):
                with pe.Fori(0, RET_HEADS) as h:
                    def head_unit(u, b, **kw):
                        unit(h * 12 + (L.n + u), L.n + u, bank[b], H, TOK, **kw).then_inc(unit_used, 1)

                    for u in range(4):
                        if u == 1:
                            pe.wait_ge(L.ors_ready, h + 1)
                        else:
                            pe.wait_ge(L.y_ready, h * ET + (2 if u == 0 else u + 1))
                        head_unit(u, u, first_of=q if u == 0 else None)
                    for s in range(4):
                        take(h * 12 + (L.n + 4 + s))
                        for kk in range(2):
                            k = 2 * s + kk
                            for tb in range(4):
                                last = three(bank[4 + tb][:, :], tuple(t[:, k, tb * P:tb * P + P] for t in H),
                                             weight(L.n + s, kk * 512, kk * 512 + 512), k == 0, k == KT - 1)
                                if k == KT - 1 and tb < 3:
                                    last.then_inc(L.v_done, 1)
                        last.then_inc(unit_used, 1)
                    pe.wait_ge(L.rot_ready, h * 2 + 2)
                    pe.wait_ge(L.zcopy_ready, h * 4 + 4)
                    for kb in range(4):
                        dst, w = (bank[0][:, kb * SEQ:kb * SEQ + SEQ], SEQ) if kb < 2 else (bank[kb - 1][:, :], TOK)
                        for d in range(2):
                            last = mm(dst, rq[:, 2 + d, kb * P:kb * P + P], rq[:, d, 0:w], d == 0, d == 1)
                        if kb:
                            last.then_inc(L.s_done, 1)
                    head_unit(8, 3)
                    pe.wait_ge(L.sT_ready, h * 3 + 3)
                    head_unit(9, 0)
                    pe.wait_ge(L.v_act, h * 2 + 2)
                    pe.wait_ge(L.v_dve, h * 2 + 2)
                    for e in range(ET):
                        for j, kb in enumerate((2, 3, 0, 1)):
                            mov, w = (sT[:, 0, kb * SEQ:kb * SEQ + SEQ], SEQ) if kb < 2 else (sT[:, kb - 1, :], TOK)
                            last = mm(bank[4 + e][:, 0:w], rv[:, kb, e * P:e * P + P], mov, j == 0, j == 3)
                        last.then_inc(L.o_done, 1)
                    head_unit(10, 2)
                    for e in range(ET):
                        pe.wait_ge(L.osq_ready, h * ET + (e + 1))
                        mm(bank[1][:, :], ones[:, :], tmp[:, e % 2, :], e == 0, e == ET - 1).then_inc(L.oms_done, 1)
                    pe.wait_ge(L.y_ready, h * ET + (ET + 1))
                    head_unit(11, 3)

            def ffn(L, q):
                n, li = L.nf, L.li
                ada = li + 1 < layers
                with pe.Fori(0, JT // 2) as i:
                    for s in range(2):
                        pe.wait_ge(L.u_free, i * 2 + (s + 1))
                        for g in range(2):
                            unit(i * 4 + (n + 2 * s + g), n + 2 * s + g, bank[2 * s + g], H, L.W,
                                 first_of=q if s + g == 0 else None).then_inc(unit_used, 1)
                        if ada:
                            for r in range(2):
                                ada_step(li + 1, i * 4 + (2 * s + r), r)
                if ada:
                    for a in range(2 * JT, MOD):
                        ada_step(li + 1, a, a % 2)
                    pe.wait_ge(mod_ready, li + 2)
                n += 2 * JT
                lead = (JT // 2) % 4
                for half in range(2):
                    banks = bank[4:8] if half == 0 else bank[0:4]

                    def step(n_at, slot, k_at, first, signal):
                        take(n_at)
                        for kk in range(2):
                            pe.wait_ge(L.u_lo_ready, JT if half else k_at + (kk + 1))
                            mov = tuple(t[:, bass.ds(k_at + kk, 1), 0:L.W].rearrange("p a n -> p (a n)")
                                        for t in (u_hi, u_lo))
                            for m in range(4):
                                last = three(banks[m][:, 0:L.W],
                                             weight(slot, kk * 512 + m * P, kk * 512 + m * P + P),
                                             mov, first and kk == 0, True, skip_group_check=True)
                                if signal and kk == 1 and m < 3:
                                    last.then_inc(L.out_done, 1)
                        last.then_inc(unit_used, 1)

                    for s in range(lead):
                        step(n + s, n + s, 2 * s, s == 0, False)
                    with pe.Fori(0, JT // 8) as i:
                        for s in range(4):
                            step(i * 4 + (n + lead + s), n + lead + s, i * 8 + 2 * (lead + s), False, s == 3)
                    n += JT // 2

            pe.wait_ge(cond_ready, 1)
            with pe.Fori(0, MOD // 2) as i:
                for r in range(2):
                    ada_step(0, i * 2 + r, r)
            pe.wait_ge(consts, 3)
            for L in plan:
                norm(2 * L.li, TOK)
                if L.kind == 1:
                    retention(L, 2 * L.li)
                else:
                    values(L, 2 * L.li)
                    attention(L)
                project(L, KT * (2 * L.li + 1))
                norm(2 * L.li + 1, L.W)
                ffn(L, 2 * L.li + 1)
            norm(NORMS, plan[-1].W)

        @block.scalar
        def _(act):
            own = Links(act, act_own)

            def conv(c, i=0, stride=0):
                if c >= UN:
                    return
                r = c % RING
                act.wait_ge(raw_loaded[r], i * (16 * stride // RING) + 16 * (c // RING + 1))
                if isinstance(i, int) and c + stride * i >= RING or not isinstance(i, int):
                    assert isinstance(i, int) or c >= RING
                    act.wait_ge(unit_used, i * stride + (c - RING + 1))
                nc.scalar.activation(w_hi[:, r, :], w_raw[:, r, :], ACT.Copy).then_inc(hi_ready, 1)

            def convs(c, count):
                count = min(count, UN - c)
                lead = count % RING
                for j in range(lead):
                    conv(c + j)
                if count >= RING:
                    with act.Fori(0, count // RING) as i:
                        for j in range(RING):
                            conv(c + lead + j, i, RING)

            def ada_load(la, a, slot):
                if not (la == 0 and isinstance(a, int) and a < 2):
                    act.wait_ge(ada_done, a + (MOD * la - 1))
                act.dma_start(ada_raw[:, slot, :], ada_w[bass.ds(a + MOD * la, 1)].rearrange("a p n -> (a p) n"))\
                   .then_inc(ada_loaded[slot], 16)

            def square(e, m, W, slot):
                act.wait_ge(x_new, e)
                src = xT[:, m, 0:W] if isinstance(m, int) else xT[:, bass.ds(m, 1), 0:W].rearrange("p a n -> p (a n)")
                nc.scalar.activation(tmp[:, slot, 0:W], src, ACT.Square).then_inc(sq_ready, 1)

            def rsqrt(W, src, count, ready):
                own(nc.scalar.activation(lnm[:, 0:W], src, ACT.Ln, bias=eps_c[:, 0:1], scale=1.0 / count))
                nc.scalar.activation(rstd[:, 0:W], lnm[:, 0:W], ACT.Exp, scale=-0.5).then_inc(ready, 1)

            def norm(q, L, which, W):
                act.wait_ge(ms_done, q + 1)
                rsqrt(W, bank[7][:, 0:W], D, rstd_ready)
                if L is None:
                    return
                for m in range(KT):
                    act.wait_ge(norm_t, q * KT + m + 1)
                    for c in range(W // SEQ):
                        last = nc.scalar.activation(h_hi[:, m, c * SEQ:c * SEQ + SEQ],
                                                    tmp[:, m % 2, c * SEQ:c * SEQ + SEQ], ACT.Identity,
                                                    bias=mod[:, L.par, 3 * KT * which + m, c:c + 1])
                    last.then_inc(h_hi_ready, 1)

            def values(L):
                def half(i):
                    for s in range(4):
                        conv(L.n + AHEAD + s, i, 4)
                    for tb in (0, 2):
                        act.wait_ge(L.v_done, i * 3 + (tb + 1))
                        nc.scalar.activation(v_all[:, tb, bass.ds(i * 512, 512)], bank[tb][:, :], ACT.Copy)\
                            .then_inc(L.v_act, 1)

                if L.n:
                    with act.Fori(0, 2) as i:
                        half(i)
                else:
                    half(0)
                    half(1)

            def attention(L):
                n = L.n + KT

                def exps(t):
                    for j in range(L.banks):
                        sub = j % 2
                        st = n_st if L.na else d_st
                        act.wait_ge(L.negmax, t * L.banks + (j + 1))
                        if j < 4:
                            dst = (n_x if L.na else e_x)[:, j // 2, sub, :]
                            col = 4 * sub + j // 2
                            last = nc.scalar.activation(dst, bank[j][:, :], ACT.Exp, bias=st[:, 0, col:col + 1],
                                                        accum_out=st[:, 1, col:col + 1])
                        else:
                            for qb in range(2):
                                dst = (n_z if L.na else e_z)[:, sub, qb, :]
                                col = 4 * sub + 2 + qb
                                last = nc.scalar.activation(dst, bank[j][:, qb * CTX:qb * CTX + CTX], ACT.Exp,
                                                            bias=st[:, 0, col:col + 1],
                                                            accum_out=st[:, 1, col:col + 1])
                        last.then_inc(L.e_ready, 1)

                def finish(t):
                    act.wait_ge(L.v_dve, 4)
                    nc.scalar.activation(v_st[:, :, :], v_all[:, :, bass.ds(t * P, P)], ACT.Copy)\
                        .then_inc(L.vst_ready, 1)
                    per = L.groups // (2 if L.na else 1)
                    for g in range(L.groups):
                        act.wait_ge(L.t_done, t * L.groups + (g + 1))
                        dst = nT[:, g // per, g % per, :] if L.na else aT[:, g, :]
                        nc.scalar.activation(dst, bank[g % per][:, :], ACT.Copy).then_inc(L.aT_ready, 1)
                    act.wait_ge(L.pv_done, t + 1)
                    o = bank[6][:, 0:L.W]
                    y = y_hi[:, bass.ds(t, 1), 0:L.W].rearrange("p a n -> p (a n)")
                    if L.na:
                        nc.scalar.activation(y, o, ACT.Copy).then_inc(L.y_hi_ready, 1)
                    else:
                        nc.scalar.activation(tmp[:, 1, 0:L.W], o, ACT.Square).then_inc(L.osq_ready, 1)
                        act.wait_ge(L.oms_done, t + 1)
                        rsqrt(L.W, bank[7][:, 0:L.W], 2 * DA_DIM, L.ors_ready)
                        act.wait_ge(L.y_ready, t + 1)
                        nc.scalar.activation(y, tmp[:, 0, 0:L.W], ACT.Copy).then_inc(L.y_hi_ready, 1)

                def bias_load(t, slot):
                    row = GRID_W * RPB_PAD
                    for sub in range(2):
                        for qr in range(ROWS):
                            src = bass.AP(tensor=rpb_skew.tensor, offset=(ROWS - 1 - qr) * row + GRID_W - 1,
                                          ap=[[7 * row, NA_HEADS], [RPB_PAD - 1, GRID_W], [row, ROWS], [1, GRID_W]])
                            lo = GRID_W * (qr % 2)
                            dst = bias[lo:lo + GRID_W, slot, sub, qr // 2, :].rearrange("p (r k) -> p r k", k=GRID_W)
                            act.dma_start(dst, src[bass.ds(t * 2 + sub, 1)].rearrange("a c r k -> (a c) r k"))\
                               .then_inc(bias_in[slot], 16)

                def tile(t, c, i, place, slot):
                    if place:
                        exps(t - 1)
                    if L.na:
                        bias_load(t, slot)
                    conv(c + AHEAD, i, 4)
                    conv(c + AHEAD + 1, i, 4)
                    if L.na:
                        act.wait_ge(unit_used, t * 2 + (n + 1))
                        nc.scalar.activation(qT[:, :], bank[6][:, :], ACT.Copy, scale=NA_DIM ** -0.5)\
                            .then_inc(L.qk_act, 1)
                    else:
                        for x, (b, dst, scale) in enumerate(((bank[6], qT, DA_DIM ** -0.5), (bank[7], kT, 1.0))):
                            act.wait_ge(unit_used, t * 2 + (n + 1 + x))
                            last = nc.scalar.activation(qk_raw[:, x, :], b[:, 0:SEQ], ACT.Copy)
                            if x or L.zq:
                                last = nc.scalar.activation(dst[:, SEQ:TOK], b[:, SEQ:TOK], ACT.Copy, scale=scale)
                            last.then_inc(L.qk_act, 1)
                    if place:
                        finish(t - 1)

                tile(0, n, 0, False, 0)
                tile(1, n + 2, 0, True, 1)
                with own.loop((KT - 2) // 2, 0 if L.na else 2) as i:
                    for s in range(2):
                        tile(i * 2 + (2 + s), n + 4 + 2 * s, i, True, s)
                exps(KT - 1)
                finish(KT - 1)

            def project(L, e0):
                if L.kind != 1:
                    n = L.n + 3 * KT
                    with act.Fori(0, 2) as i:
                        for s in range(4):
                            conv(n + AHEAD + s, i, 4)
                            square(i * 4 + (e0 + s + 1), i * 4 + s, L.W, s % 2)
                else:
                    n = L.n + 12 * RET_HEADS
                    with act.Fori(0, 4) as i:
                        for s in range(2):
                            conv(n + AHEAD + 2 * s, i, 4)
                            conv(n + AHEAD + 2 * s + 1, i, 4)
                            square(i * 2 + (e0 + s + 1), i * 2 + s, L.W, s)

            def retention(L):
                with own.loop(RET_HEADS, 1) as h:
                    def hconv(*us):
                        for u in us:
                            conv(L.n + AHEAD + u, h, 12)

                    act.wait_ge(L.darg_ready, h + 1)
                    nc.scalar.activation(decay[:, :, 1, :], darg[:, :, :], ACT.Exp)
                    nc.scalar.activation(decay[:, :, 0, :], ret_exp[:, 2, :, :], ACT.Exp, scale=lg_cur[:, 0:1])
                    nc.scalar.activation(lnm[:, :].rearrange("p (a n) -> p a n", a=2), ret_exp[:, 3, :, :], ACT.Exp,
                                         scale=lg_cur[:, 1:2]).then_inc(L.dexp_ready, 1)
                    for u in range(4):
                        hconv(u)
                        act.wait_ge(unit_used, h * 12 + (L.n + u + 1))
                        nc.scalar.activation(rq[:, u, SEQ:TOK], bank[u][:, SEQ:TOK], ACT.Copy)\
                            .then_inc(L.zcopy_ready, 1)
                    hconv(4, 5, 6, 7)
                    for tb in (0, 2):
                        act.wait_ge(L.v_done, h * 3 + (tb + 1))
                        nc.scalar.activation(rv[:, tb, :], bank[4 + tb][:, :], ACT.Copy).then_inc(L.v_act, 1)
                    hconv(8, 9)
                    for e in range(ET):
                        act.wait_ge(L.o_done, h * ET + (e + 1))
                        if e >= 2:
                            act.wait_ge(L.oms_done, h * ET + (e - 1))
                        nc.scalar.activation(tmp[:, e % 2, :], bank[4 + e][:, :], ACT.Square).then_inc(L.osq_ready, 1)
                    hconv(10, 11)
                    act.wait_ge(L.oms_done, h * ET + ET)
                    rsqrt(TOK, bank[1][:, :], RET_V, L.ors_ready)

                    def gate(e):
                        if e == 0:
                            act.wait_ge(L.ors_ready, h + 2)
                        act.wait_ge(unit_used, h * 12 + (L.n + 9 + e))
                        nc.scalar.activation(gate_buf(e), bank[(3, 0, 2, 3)[e]][:, :], ACT.Silu).then_inc(L.silu_g, 1)

                    def high(e):
                        act.wait_ge(L.y_ready, h * ET + (ET + e + 1))
                        nc.scalar.activation(ry_hi[:, bass.ds(h * ET + e, 1), :].rearrange("p a n -> p (a n)"),
                                             tmp[:, e % 2, :], ACT.Copy).then_inc(L.y_hi_ready, 1)

                    gate(0)
                    gate(1)
                    high(0)
                    gate(2)
                    high(1)
                    gate(3)
                    high(2)
                    high(3)

            def ffn(L, e0):
                n, li = L.nf, L.li
                ada = li + 1 < layers
                if ada:
                    for a in range(2):
                        ada_load(li + 1, a, a)
                with act.Fori(0, JT // 2) as i:
                    for s in range(2):
                        conv(n + AHEAD + 2 * s, i, 4)
                        conv(n + AHEAD + 2 * s + 1, i, 4)
                        act.wait_ge(unit_used, i * 4 + (n + 2 * s + 2))
                        nc.scalar.activation(lnm[:, 0:L.W], bank[2 * s][:, 0:L.W], ACT.Silu)\
                            .then_inc(L.silu_ready, 1)
                        act.wait_ge(L.u_free, i * 2 + (s + 3))
                        nc.scalar.activation(u_hi[:, bass.ds(i * 2 + s, 1), 0:L.W].rearrange("p a n -> p (a n)"),
                                             tmp[:, s, 0:L.W], ACT.Copy).then_inc(L.u_hi_ready, 1)
                        if ada:
                            for r in range(2):
                                ada_load(li + 1, i * 4 + (2 * s + 2 + r), r)
                if ada:
                    for a in range(2 * JT + 2, MOD):
                        ada_load(li + 1, a, a % 2)
                n += 2 * JT
                convs(n + AHEAD, JT // 2)
                lead = (JT // 2) % 4
                convs(n + JT // 2 + AHEAD, lead)
                for m in range(4):
                    square(e0 + m + 1, m, L.W, m % 2)
                convs(n + JT // 2 + AHEAD + lead, JT // 2 - lead)
                for m in range(4, 8):
                    square(e0 + m + 1, m, L.W, m % 2)

            for a in range(2):
                ada_load(0, a, a)
            act.wait_ge(small_in, SMALL)
            nc.scalar.activation(cond[:, :, :], cond_raw[:, :, :], ACT.Silu).then_inc(cond_ready, 1)
            conv(0)
            conv(1)
            act.wait_ge(consts, 3)
            act.wait_ge(lam_sums, 1)
            nc.scalar.activation(lam_sum[:, :, :], lam_sum[:, :, :], ACT.Exp).then_inc(lam_exps, 1)
            act.wait_ge(log_abs, 1)
            own(nc.scalar.activation(lg_t[:, 1, :], lg_t[:, 0, :], ACT.Exp, scale=-1.0))
            nc.scalar.activation(lg_t[:, 2, :], lg_t[:, 1, :], ACT.Ln, bias=one_c[:, 0:1]).then_inc(log_parts, 1)
            with act.Fori(0, MOD // 2 - 1) as i:
                for r in range(2):
                    ada_load(0, i * 2 + (2 + r), r)
            for m in range(KT):
                if m >= 2:
                    act.wait_ge(ssum_step, m - 1)
                square(KT, m, TOK, m % 2)
            for L in plan:
                norm(2 * L.li, L, 0, TOK)
                if L.kind == 0:
                    act.dma_start(da_rope[:, :, :], da_rope_in).then_inc(table_in, 16)
                    values(L)
                    attention(L)
                elif L.kind == 1:
                    act.dma_start(ret_rope[:, :, :], ret_rope_in).then_inc(table_in, 16)
                    act.dma_start(ret_exp[:, :, :, :], ret_exp_in).then_inc(table_in, 16)
                    retention(L)
                else:
                    act.dma_start(na_mask[:, :], na_mask_in).then_inc(table_in, 16)
                    act.wait_ge(rpb_zero, 1)
                    pad = GRID_W - NA_KW
                    act.dma_start(rpb_rows[:, pad:pad + RPB_W], rpb_in).then_inc(skew_in, 16)
                    act.wait_ge(skew_in, 16)
                    act.dma_start(rpb_skew, rpb_rows[:, :].unsqueeze(1).to_broadcast([7 * NA_HEADS, GRID_W, RPB_PAD]))\
                       .then_inc(skew_out, 16)
                    values(L)
                    act.wait_ge(skew_out, 16)
                    attention(L)
                project(L, KT * (2 * L.li + 1))
                norm(2 * L.li + 1, L, 1, L.W)
                ffn(L, KT * (2 * L.li + 2))
            norm(NORMS, None, 0, plan[-1].W)

        @block.vector
        def _(dve):
            own = Links(dve, dve_own)
            V = nc.vector

            def row(t, m, W):
                return t[:, m, 0:W] if isinstance(m, int) else t[:, bass.ds(m, 1), 0:W].rearrange("p a n -> p (a n)")

            def gate_of(L, which, m, c):
                at = m + KT * which
                if isinstance(m, int):
                    return mod[:, L.par, at, c:c + 1]
                return mod[:, L.par, bass.ds(at, 1), c:c + 1].rearrange("p a c -> p (a c)")

            def modulation(la):
                par = la % 2
                dve.wait_ge(ada_done, MOD * (la + 1))
                own(V.tensor_tensor(out=mod[:, par, :, :], in0=bank[6][:, 0:2 * MOD].rearrange("p (m c) -> p m c", c=2),
                                    in1=bias_ada[:, la, :].unsqueeze(2).to_broadcast([P, MOD, 2]), op=ALU.add))
                for j in range(2):
                    a = KT * (3 * j + 1)
                    last = V.scalar_tensor_tensor(out=amp[:, par, j, :, :], in0=mod[:, par, a:a + KT, :], scalar=1.0,
                                                  in1=gain[:, la, j, :].unsqueeze(2).to_broadcast([P, KT, 2]),
                                                  op0=ALU.add, op1=ALU.mult)
                last.then_inc(mod_ready, 1)
                dve.wait_ge(mod_ready, la + 1)

            def residual(L, which, src, m, W):
                for c in range(W // SEQ):
                    x = row_part(m, c)
                    last = V.scalar_tensor_tensor(out=x, in0=src[:, c * SEQ:c * SEQ + SEQ],
                                                  scalar=gate_of(L, which, m, c), in1=x, op0=ALU.mult, op1=ALU.add)
                last.then_inc(x_new, 1)

            def row_part(m, c):
                if isinstance(m, int):
                    return xT[:, m, c * SEQ:c * SEQ + SEQ]
                return xT[:, bass.ds(m, 1), c * SEQ:c * SEQ + SEQ].rearrange("p a n -> p (a n)")

            def add_square(e, slot, W, first=False):
                dve.wait_ge(sq_ready, e)
                if not first:
                    dve.wait_ge(ssum_step, e - 1)
                V.tensor_tensor(out=ssum[:, 0:W], in0=ssum[:, 0:W], in1=tmp[:, slot, 0:W], op=ALU.add)\
                    .then_inc(ssum_step, 1)

            def norm(q, L, which, W):
                dve.wait_ge(rstd_ready, q + 1)
                own(V.memset(ssum[:, :], 0.0))

                def scaled(m):
                    if m >= 2:
                        dve.wait_ge(h_ready, q * KT + m - 1)
                    for c in range(W // SEQ):
                        last = V.scalar_tensor_tensor(out=tmp[:, m % 2, c * SEQ:c * SEQ + SEQ],
                                                      in0=xT[:, m, c * SEQ:c * SEQ + SEQ],
                                                      scalar=amp[:, L.par, which, m, c:c + 1],
                                                      in1=rstd[:, c * SEQ:c * SEQ + SEQ], op0=ALU.mult, op1=ALU.mult)
                    last.then_inc(norm_t, 1)

                def low(m):
                    dve.wait_ge(h_hi_ready, q * KT + m + 1)
                    for c in range(W // SEQ):
                        s = slice(c * SEQ, c * SEQ + SEQ)
                        last = V.scalar_tensor_tensor(out=h_lo[:, m, s], in0=tmp[:, m % 2, s],
                                                      scalar=mod[:, L.par, 3 * KT * which + m, c:c + 1],
                                                      in1=h_hi[:, m, s].bitcast(F32), op0=ALU.add, op1=ALU.subtract)
                    last.then_inc(h_ready, 1)

                scaled(0)
                for m in range(1, KT):
                    scaled(m)
                    low(m - 1)
                low(KT - 1)

            def values(L):
                with dve.Fori(0, 2) as i:
                    for tb in (1, 3):
                        if tb == 1:
                            dve.wait_ge(L.v_done, i * 3 + 2)
                        else:
                            dve.wait_ge(unit_used, i * 4 + (L.n + 4))
                        V.tensor_copy(v_all[:, tb, bass.ds(i * 512, 512)], bank[tb][:, :]).then_inc(L.v_dve, 1)

            def rotate(src, dst, table):
                for quarter in range(4):
                    a, b = 32 * quarter, 32 * (quarter ^ 1)
                    V.tensor_tensor(out=rot[a:a + 32, 0, :], in0=src[b:b + 32, :],
                                    in1=da_rope[b:b + 32, table + 1, :], op=ALU.mult)
                own(V.tensor_tensor(out=rot[:, 1, :], in0=src, in1=da_rope[:, table, :], op=ALU.mult))
                return V.tensor_tensor(out=dst, in0=rot[:, 0, :], in1=rot[:, 1, :], op=ALU.add)

            def attention(L, e0):
                n = L.n + KT

                def weights_(t, slot):
                    st = n_st if L.na else d_st
                    if L.na:
                        dve.wait_ge(bias_in[slot], t * 64 + (128 - 64 * slot))
                        b = bias[:, slot, :, :, :].rearrange("p h q (r k) -> p (h q r) k", k=GRID_W)
                        own(V.tensor_tensor(out=b, in0=b,
                                            in1=na_mask[:, :].unsqueeze(1).to_broadcast([P, 4 * ROWS, GRID_W]),
                                            op=ALU.add))
                    for j in range(L.banks):
                        sub = j % 2
                        dve.wait_ge(L.s_done, t * L.banks + (j + 1))
                        if j < 4:
                            if L.na:
                                own(V.tensor_tensor(out=bank[j][:, 0:SEQ], in0=bank[j][:, 0:SEQ],
                                                    in1=bias[:, slot, sub, j // 2, :], op=ALU.add))
                            col = 4 * sub + j // 2
                            last = V.tensor_reduce(out=st[:, 0, col:col + 1], in_=bank[j][:, :], axis=AX.X, op=ALU.max,
                                                   negate=True)
                        else:
                            last = V.tensor_reduce(out=st[:, 0, 4 * sub + 2:4 * sub + 4],
                                                   in_=bank[j][:, :].rearrange("p (q k) -> p q k", q=2), axis=AX.X,
                                                   op=ALU.max, negate=True)
                        last.then_inc(L.negmax, 1)
                    dve.wait_ge(L.e_ready, t * L.banks + L.banks)
                    cols = 4 if L.zq else 2
                    grp = [st[:, k, :].rearrange("p (s c) -> p s c", s=2)[:, :, 0:cols] for k in range(3)]
                    own(V.reciprocal(grp[2], grp[1]))
                    if L.na:
                        for sub in range(2):
                            for qb in range(4):
                                x = n_x[:, qb, sub, :] if qb < 2 else n_z[:, sub, qb - 2, :]
                                last = V.tensor_scalar(x, x, st[:, 2, 4 * sub + qb:4 * sub + qb + 1], None, ALU.mult)
                    else:
                        own(V.tensor_scalar(st[:, 3, 0:cols], st[:, 2, 4:4 + cols], neg_lam[:, L.da:L.da + 1], None,
                                            ALU.mult))
                        parts = [(a_x[:, qb, :], e_x[:, qb, 0, :], e_x[:, qb, 1, :]) if qb < 2 else
                                 (a_z[:, qb - 2, :], e_z[:, 0, qb - 2, :], e_z[:, 1, qb - 2, :])
                                 for qb in range(cols)]
                        for qb, (a, x0, x1) in enumerate(parts):
                            ins = V.tensor_scalar(a, x0, st[:, 2, qb:qb + 1], None, ALU.mult)
                            if qb == cols - 1:
                                own(ins)
                        for qb, (a, x0, x1) in enumerate(parts):
                            last = V.scalar_tensor_tensor(out=a, in0=x1, scalar=st[:, 3, qb:qb + 1], in1=a,
                                                          op0=ALU.mult, op1=ALU.add)
                    last.then_inc(L.a_ready, 1)

                def finish(t):
                    if not L.na:
                        dve.wait_ge(L.ors_ready, t + 1)
                        V.scalar_tensor_tensor(out=tmp[:, 0, 0:L.W], in0=bank[6][:, 0:L.W],
                                               scalar=subln[:, L.da:L.da + 1], in1=rstd[:, 0:L.W], op0=ALU.mult,
                                               op1=ALU.mult).then_inc(L.y_ready, 1)
                    dve.wait_ge(L.y_hi_ready, t + 1)
                    V.tensor_tensor(out=row(y_lo, t, L.W), in0=bank[6][:, 0:L.W] if L.na else tmp[:, 0, 0:L.W],
                                    in1=row(y_hi, t, L.W), op=ALU.subtract).then_inc(L.y_lo_ready, 1)

                def tile(t, place, slot):
                    if place:
                        weights_(t - 1, 1 - slot)
                    if L.na:
                        dve.wait_ge(unit_used, t * 2 + (n + 2))
                        V.tensor_copy(kT[:, :], bank[7][:, :]).then_inc(L.qk_dve, 1)
                    else:
                        dve.wait_ge(L.qk_act, t * 2 + 1)
                        rotate(qk_raw[:, 0, :], qT[:, 0:SEQ], 0).then_inc(L.qk_dve, 1)
                        dve.wait_ge(L.qk_act, t * 2 + 2)
                        dve.wait_ge(L.qk_dve, t * 2 + 1)
                        rotate(qk_raw[:, 1, :], kT[:, 0:SEQ], 2).then_inc(L.qk_dve, 1)
                    if place:
                        finish(t - 1)

                tile(0, 0, 0)
                tile(1, 1, 1)
                per_tile = (1 + 4 + 1) if L.na else 3 + 2
                with own.loop((KT - 2) // 2, 2 * per_tile) as i:
                    for s in range(2):
                        tile(i * 2 + (2 + s), 1, s)
                weights_(KT - 1, 1)
                finish(KT - 1)

            def project(L, e0):
                per, body = (4, 4) if L.kind != 1 else (2, 2)
                n = L.n + (3 * KT if L.kind != 1 else 12 * RET_HEADS)
                with dve.Fori(0, KT // body) as i:
                    for s in range(body):
                        used = s + 1 if L.kind != 1 else 2 * s + 2
                        dve.wait_ge(unit_used, i * 4 + (n + used))
                        residual(L, 2, bank[s], i * body + s, L.W)
                        add_square(i * body + (e0 + s + 1), s % 2, L.W)

            def retention(L):
                with own.loop(RET_HEADS, 5 + ET) as h:
                    own(V.tensor_copy(lg_cur[:, :].unsqueeze(2), log_g[:, :, bass.ds(h, 1)]))
                    own(V.tensor_scalar(darg[:, :, :], ret_exp[:, 1, :, :], lg_cur[:, 1:2], None, ALU.mult))
                    V.scalar_tensor_tensor(out=darg[:, :, :], in0=ret_exp[:, 0, :, :], scalar=lg_cur[:, 0:1],
                                           in1=darg[:, :, :], op0=ALU.mult, op1=ALU.add).then_inc(L.darg_ready, 1)
                    dve.wait_ge(L.dexp_ready, h + 1)
                    own(V.tensor_tensor(out=decay[:, :, 0, :], in0=decay[:, :, 0, :],
                                        in1=lnm[:, :].rearrange("p (a n) -> p a n", a=2), op=ALU.add))
                    half = [tmp[:, j // 2, SEQ * (j % 2):SEQ * (j % 2) + SEQ] for j in range(4)]
                    for x in range(2):
                        dve.wait_ge(L.zcopy_ready, h * 4 + (2 * x + 2))
                        if x:
                            dve.wait_ge(L.rot_ready, h * 2 + 1)
                        for j, (b, tab) in enumerate(((0, 0), (1, 1), (0, 1), (1, 0))):
                            ins = V.tensor_tensor(out=half[j], in0=bank[2 * x + b][:, 0:SEQ], in1=ret_rope[:, tab, :],
                                                  op=ALU.mult)
                        own(ins)
                        V.tensor_tensor(out=rq[:, 2 * x, 0:SEQ], in0=half[0], in1=half[1], op=ALU.subtract)
                        V.tensor_tensor(out=rq[:, 2 * x + 1, 0:SEQ], in0=half[2], in1=half[3], op=ALU.add)\
                            .then_inc(L.rot_ready, 1)
                    for tb in (1, 3):
                        if tb == 1:
                            dve.wait_ge(L.v_done, h * 3 + 2)
                        else:
                            dve.wait_ge(unit_used, h * 12 + (L.n + 8))
                        V.tensor_copy(rv[:, tb, :], bank[4 + tb][:, :]).then_inc(L.v_dve, 1)
                    for g in range(3):
                        dve.wait_ge(L.s_done, h * 3 + (g + 1))
                        dec = decay[:, :, 1, :] if g == 0 else decay[:, g - 1, :, :]
                        V.scalar_tensor_tensor(out=sT[:, g, :].rearrange("p (a n) -> p a n", a=2),
                                               in0=bank[g][:, :].rearrange("p (a n) -> p a n", a=2),
                                               scalar=RET_QK ** -0.5, in1=dec, op0=ALU.mult, op1=ALU.mult)\
                            .then_inc(L.sT_ready, 1)

                    def gated(e):
                        dve.wait_ge(L.ors_ready, h + 2)
                        if e:
                            dve.wait_ge(L.y_ready, h * ET + (ET + e))
                        own(V.tensor_tensor(out=ssum[:, :], in0=bank[4 + e][:, :], in1=rstd[:, :], op=ALU.mult))
                        dve.wait_ge(L.silu_g, h * ET + (e + 1))
                        V.tensor_tensor(out=tmp[:, e % 2, :], in0=ssum[:, :], in1=gate_buf(e), op=ALU.mult)\
                            .then_inc(L.y_ready, 1)

                    def low(e):
                        dve.wait_ge(L.y_hi_ready, h * ET + (e + 1))
                        V.tensor_tensor(out=row(ry_lo, h * ET + e, TOK), in0=tmp[:, e % 2, :],
                                        in1=row(ry_hi, h * ET + e, TOK), op=ALU.subtract).then_inc(L.y_lo_ready, 1)

                    gated(0)
                    for e in range(1, ET):
                        gated(e)
                        low(e - 1)
                    low(ET - 1)
                own(V.memset(ssum[:, :], 0.0))

            def ffn(L, e0):
                n, li = L.nf, L.li
                ada = li + 1 < layers
                dve.sem_inc(L.u_free, 2)
                with dve.Fori(0, JT // 2) as i:
                    for s in range(2):
                        dve.wait_ge(L.silu_ready, i * 2 + (s + 1))
                        V.tensor_tensor(out=tmp[:, s, 0:L.W], in0=bank[2 * s + 1][:, 0:L.W], in1=lnm[:, 0:L.W],
                                        op=ALU.mult).then_inc(L.u_free, 1)
                        dve.wait_ge(L.u_hi_ready, i * 2 + (s + 1))
                        V.tensor_tensor(out=row(u_lo, i * 2 + s, L.W), in0=tmp[:, s, 0:L.W],
                                        in1=row(u_hi, i * 2 + s, L.W), op=ALU.subtract).then_inc(L.u_lo_ready, 1)
                if ada:
                    modulation(li + 1)
                n += 2 * JT
                for half in range(2):
                    banks = bank[4:8] if half == 0 else bank[0:4]
                    n += JT // 2
                    for m in range(4):
                        if m < 3:
                            dve.wait_ge(L.out_done, 6 * half + 3 + m + 1)
                        else:
                            dve.wait_ge(unit_used, n)
                        residual(L, 5, banks[m], 4 * half + m, L.W)
                        if m:
                            add_square(e0 + 4 * half + m, (m - 1) % 2, L.W)
                    add_square(e0 + 4 * half + 4, 1, L.W)

            dve.sem_inc(x_new, KT)
            for L in plan:
                if L.kind == 1:
                    dve.sem_inc(L.y_ready, ET)
                    dve.sem_inc(L.ors_ready, 1)
            own(V.memset(ssum[:, :], 0.0))
            dve.wait_ge(small_in, SMALL)
            pairs = lam_sb[:, :, :, :].rearrange("p l (a b) d -> p l a b d", b=2)
            own(V.tensor_tensor(out=lam_pr[:, :, :, :], in0=pairs[:, :, :, 0, :], in1=pairs[:, :, :, 1, :], op=ALU.mult))
            V.tensor_reduce(out=lam_sum[:, :, :], in_=lam_pr[:, :, :, :], axis=AX.X, op=ALU.add).then_inc(lam_sums, 1)
            V.scalar_tensor_tensor(out=lg_t[:, 0, :], in0=logit[:, :], scalar=-1.0, in1=logit[:, :], op0=ALU.mult,
                                   op1=ALU.max).then_inc(log_abs, 1)
            own(V.tensor_scalar(lg_t[:, 3, :], logit[:, :], 0.0, None, ALU.min))
            dve.wait_ge(lam_exps, 1)
            own(V.tensor_tensor(out=neg_lam[:, :].unsqueeze(2), in0=lam_sum[:, :, 1:2], in1=lam_sum[:, :, 0:1],
                                op=ALU.subtract))
            da_layers = [li for li in range(DEPTH) if KINDS[li] == 0]
            for j, li in enumerate(da_layers):
                init = 0.8 - 0.6 * math.exp(-0.3 * li)
                V.tensor_scalar(neg_lam[:, j:j + 1], neg_lam[:, j:j + 1], -init, None, ALU.add)
                own(V.tensor_scalar(subln[:, j:j + 1], subln[:, j:j + 1], 1.0 - init, None, ALU.mult))
            dve.wait_ge(log_parts, 1)
            own(V.tensor_tensor(out=log_g[:, :, :], in0=lg_t[:, 3, :].rearrange("p (a h) -> p a h", a=2),
                                in1=lg_t[:, 2, :].rearrange("p (a h) -> p a h", a=2), op=ALU.subtract))
            for m in range(KT):
                add_square(m + 1, m % 2, TOK, first=m == 0)
            modulation(0)
            tables = 0
            for L in plan:
                if L.kind == 2:
                    dve.wait_ge(rstd_ready, 2 * L.li + 1)
                    V.memset(rpb_rows[:, :], 0.0).then_inc(rpb_zero, 1)
                norm(2 * L.li, L, 0, TOK)
                tables += 2 if L.kind == 1 else 1
                dve.wait_ge(table_in, 16 * tables)
                if L.kind == 1:
                    retention(L)
                else:
                    values(L)
                    attention(L, 0)
                project(L, KT * (2 * L.li + 1))
                norm(2 * L.li + 1, L, 1, L.W)
                ffn(L, KT * (2 * L.li + 2))
            dve.wait_ge(rstd_ready, NORMS + 1)
            for m in range(KT):
                if layers == DEPTH:
                    V.scalar_tensor_tensor(out=xT[:, m, 0:SEQ], in0=xT[:, m, 0:SEQ], scalar=gain_f[:, m:m + 1],
                                           in1=rstd[:, 0:SEQ], op0=ALU.mult, op1=ALU.mult).then_inc(fin_ready, 1)
                else:
                    dve.sem_inc(fin_ready, 1)


def _tall(w, c):
    k = w.shape[0] // P
    u = w[:, c:c + P].reshape(k // KT, KT, P, P)
    return list(u.transpose(0, 2, 1, 3).reshape(k // KT, P, KT * P))


def _wide(w, c):
    u = w[:, c:c + 512].reshape(w.shape[0] // (2 * P), 2, P, 512)
    return list(u.transpose(0, 2, 1, 3).reshape(-1, P, 1024))


def _stream(inputs, layers):
    units = []
    seen = {0: 0, 1: 0, 2: 0}
    for li in range(layers):
        kind = KINDS[li]
        at = seen[kind]
        seen[kind] += 1
        if kind == 1:
            w, wo = inputs["ret_w_in"][at], inputs["ret_w_o"][at]
            for h in range(RET_HEADS):
                for c in (h * 2 * P, h * 2 * P + P, D + h * 2 * P, D + h * 2 * P + P):
                    units += _tall(w, c)
                units += _wide(w, 2 * D + h * RET_V)
                for e in range(ET):
                    units += _tall(w, 4 * D + h * RET_V + e * P)
        else:
            w, wo = (inputs["da_w_qkv"][at], inputs["da_w_o"][at]) if kind == 0 else                 (inputs["na_w_qkv"][at], inputs["na_w_o"][at])
            units += _wide(w, 2 * D) + _wide(w, 2 * D + 512)
            for t in range(KT):
                units += _tall(w, t * P) + _tall(w, D + t * P)
        for m in range(KT):
            units += _tall(wo, m * P)
        w = inputs["ffn_in"][li]
        for j in range(JT):
            units += _tall(w, j * P) + _tall(w, HIDDEN + j * P)
        units += _wide(inputs["ffn_out"][li], 0) + _wide(inputs["ffn_out"][li], 512)
    return np.stack(units)


def kernel(layers=DEPTH, **inputs):
    import concourse.bacc as _bacc
    from concourse.bass_utils import run_bass_kernel_spmd as _run

    a = {k: np.asarray(v) for k, v in inputs.items()}
    arrays = {
        "xT": np.concatenate([a["x"][0], a["ctx"][0]], 0).T.reshape(KT, P, TOK).transpose(1, 0, 2),
        "cond": np.stack([a["c"][0], a["c_ctx"]], 1).reshape(KT, P, 2).transpose(1, 0, 2),
        "weights": _stream(a, layers),
        "ada_w": a["w_ada"].reshape(DEPTH, KT, P, MOD, P).transpose(0, 3, 2, 1, 4).reshape(DEPTH * MOD, P, D),
        "ada_b": a["b_ada"].reshape(DEPTH, MOD, P).transpose(2, 0, 1),
        "gains": a["norm_g"].reshape(DEPTH, 2, KT, P).transpose(3, 0, 1, 2),
        "final_g": a["final_g"].reshape(KT, P).T,
        "lam": a["da_lambda"],
        "subln": a["da_subln"].T,
        "decay": a["ret_decay"][0].reshape(-1),
        "rpb": a["na_rpb"][0][:, NA_KH - ROWS:NA_KH + ROWS - 1, :].reshape(NA_HEADS * 7, RPB_W),
        **shape_tables(),
    }
    arrays = {f"in_{k}": np.ascontiguousarray(v) for k, v in arrays.items()}
    nc = _bacc.Bacc("TRN2", target_bir_lowering=False, num_devices=1)
    args = [nc.dram_tensor(k, v.shape, mybir.dt.from_np(v.dtype), kind="ExternalInput").ap()
            for k, v in arrays.items()]
    W = SEQ if layers == DEPTH else TOK
    out = nc.dram_tensor("out_x", (P, KT, W), F32, kind="ExternalOutput").ap()
    trunk(nc, *args, out, layers=layers)
    r = _run(nc, [arrays], core_ids=[0])
    got = r.results[0]["out_x"]
    return got.transpose(1, 0, 2).reshape(D, W).T.reshape(1, W, D)
```

```python
import math
from contextlib import ExitStack

import numpy as np

import concourse.bass as bass
from concourse import mybir

F32 = mybir.dt.float32
F32R = mybir.dt.float32r
F16 = mybir.dt.float16
ALU = mybir.AluOpType
ACT = mybir.ActivationFunctionType
AX = mybir.AxisListType

P = 128
D = 1024
KT = D // P
SEQ = 256
CTX = 256
TOK = SEQ + CTX
DEPTH = 4
GRID_W = 64
ROWS = SEQ // GRID_W
HIDDEN = -(-8 * D // (3 * 256)) * 256
JT = HIDDEN // P
DA_HEADS = 8
DA_DIM = D // (2 * DA_HEADS)
RET_HEADS = 4
RET_QK = D // RET_HEADS
RET_V = 2 * RET_QK
ET = RET_V // P
NA_HEADS = 16
NA_KH, NA_KW = 8, 16
NA_DIM = D // NA_HEADS
RPB_W = 2 * NA_KW - 1
RPB_PAD = 2 * GRID_W - 1
MOD = 6 * KT
EPS = 1e-6
RING = 4
AHEAD = RING
ADA_RING = 2
ADA_GROUP = 4
ADA_FIRST = 2 * KT
KINDS = [li % 3 for li in range(DEPTH)]
MIXER_UNITS = {0: 4 * KT, 1: RET_HEADS * 12 + 2 * KT, 2: 4 * KT}
FFN_UNITS = 3 * JT
UNITS = sum(MIXER_UNITS[k] + FFN_UNITS for k in KINDS)


def shape_tables():
    t = np.arange(SEQ)
    rows, cols = (t // GRID_W).astype(np.float32), (t % GRID_W).astype(np.float32)

    def angles(f):
        inv = (np.float32(10000.0) ** (-np.arange(f, dtype=np.float32) / np.float32(f))).astype(np.float32)
        return np.concatenate([inv[:, None] * rows, inv[:, None] * cols], 0).astype(np.float32)

    a = angles(DA_DIM // 4)
    half = DA_DIM // 2
    ang = np.stack([a[p % half] for p in range(P)])
    sign = np.array([1.0 if p % DA_DIM < half else -1.0 for p in range(P)], np.float32)[:, None]
    c, s = np.cos(ang), np.sin(ang) * sign
    q = np.float32(DA_DIM ** -0.5)
    da_rope = np.stack([c * q, s * q, c, s], 1).astype(np.float32)
    b = angles(RET_QK // 4)
    ret_rope = np.stack([np.cos(b), np.sin(b)], 1).astype(np.float32)
    key = (np.arange(2)[None, :, None] * P + np.arange(P)[:, None, None])
    qry = np.arange(SEQ)[None, None, :]
    ret_exp = np.stack([np.maximum(qry - key, 0), np.maximum(key - qry, 0),
                        CTX + qry - key, CTX - qry + key], 1).astype(np.float16)
    col = np.arange(GRID_W)
    cs = np.clip(col - NA_KW // 2, 0, GRID_W - NA_KW)
    ok = (col[None, :] >= cs[:, None]) & (col[None, :] < cs[:, None] + NA_KW)
    mask = np.where(ok, 0.0, -3.0e38).astype(np.float32)
    return {"da_rope": da_rope, "ret_rope": ret_rope, "ret_exp": ret_exp,
            "na_mask": np.concatenate([mask, mask], 0), "ident": np.eye(P, dtype=np.float32)}


class Links:

    def __init__(self, eng, sem):
        self.eng, self.sem, self.base, self.n = eng, sem, 0, 0

    def __call__(self, ins):
        self.n += 1
        ins.then_inc(self.sem, 1)
        self.eng.wait_ge(self.sem, self.base + self.n)

    def loop(self, trips, per):
        return _LinkedLoop(self, trips, per)


class _LinkedLoop:
    def __init__(self, links, trips, per):
        self.links, self.trips, self.per = links, trips, per
        self.start = links.n
        self.loop = links.eng.Fori(0, trips)

    def __enter__(self):
        i = self.loop.__enter__()
        self.links.base, self.links.n = i * self.per + self.start, 0
        return i

    def __exit__(self, *error):
        if error[0] is None:
            assert self.links.n == self.per, self.links.n
        self.links.base, self.links.n = 0, self.start + self.trips * self.per
        return self.loop.__exit__(*error)


class Layer:

    def __init__(self, sem, li, first_unit):
        self.li, self.kind, self.par = li, KINDS[li], li % 2
        self.n, self.nf = first_unit, first_unit + MIXER_UNITS[self.kind]
        self.zq = li < DEPTH - 1
        self.W = TOK if self.zq else SEQ
        self.na = self.kind == 2
        self.da = sum(k == 0 for k in KINDS[:li])
        self.banks = 6 if self.zq else 4
        self.groups = (3 if self.zq else 2) * (2 if self.na else 1)
        self.v_done = sem(f"v_done_{li}")
        self.v_act = sem(f"v_act_{li}")
        self.v_dve = sem(f"v_dve_{li}")
        self.s_done = sem(f"s_done_{li}")
        self.osq_ready = sem(f"osq_ready_{li}")
        self.oms_done = sem(f"oms_done_{li}")
        self.ors_ready = sem(f"ors_ready_{li}")
        self.y_ready = sem(f"y_ready_{li}")
        self.y_hi_ready = sem(f"y_hi_ready_{li}")
        self.y_lo_ready = sem(f"y_lo_ready_{li}")
        if self.kind == 1:
            self.darg_ready = sem(f"darg_ready_{li}")
            self.dexp_ready = sem(f"dexp_ready_{li}")
            self.rot_ready = sem(f"rot_ready_{li}")
            self.zcopy_ready = sem(f"zcopy_ready_{li}")
            self.sT_ready = sem(f"sT_ready_{li}")
            self.o_done = sem(f"o_done_{li}")
            self.silu_g = sem(f"silu_g_{li}")
        else:
            self.qk_dve = sem(f"qk_dve_{li}")
            self.qk_act = sem(f"qk_act_{li}")
            self.negmax = sem(f"negmax_{li}")
            self.e_ready = sem(f"e_ready_{li}")
            self.a_ready = sem(f"a_ready_{li}")
            self.t_done = sem(f"t_done_{li}")
            self.aT_ready = sem(f"aT_ready_{li}")
            self.vst_ready = sem(f"vst_ready_{li}")
            self.pv_done = sem(f"pv_done_{li}")
        self.silu_ready = sem(f"silu_ready_{li}")
        self.u_free = sem(f"u_free_{li}")
        self.u_hi_ready = sem(f"u_hi_ready_{li}")
        self.u_lo_ready = sem(f"u_lo_ready_{li}")
        self.out_done = sem(f"out_done_{li}")


def trunk(nc, xT_in, cond_in, weights, ada_w, ada_b, gains, final_g, lam_in, subln_in, decay_in,
          rpb_in, da_rope_in, ret_rope_in, ret_exp_in, na_mask_in, ident_in, out, layers=DEPTH):
    with ExitStack() as ctx:
        def sb(name, shape, dt=F32, at=ctx):
            return at.enter_context(nc.sbuf_tensor(name, shape, dt))

        def sem(name):
            return ctx.enter_context(nc.semaphore(name))

        w_raw = sb("w_raw", [P, RING, D])
        w_hi = sb("w_hi", [P, RING, D], F32R)
        w_lo = sb("w_lo", [P, RING, D], F32R)
        xT = sb("xT", [P, KT, TOK])
        h_hi = sb("h_hi", [P, KT, TOK], F32R)
        h_lo = sb("h_lo", [P, KT, TOK], F32R)
        mod = sb("mod", [P, 2, MOD, 2])
        amp = sb("amp", [P, 2, 2, KT, 2])
        ada_sum = sb("ada_sum", [P, ADA_GROUP, 2, 2])
        bias_ada = sb("bias_ada", [P, DEPTH, MOD])
        gain = sb("gain", [P, DEPTH, 2, KT])
        gain_f = sb("gain_f", [P, KT])
        eps_c = sb("eps_c", [P, 1])
        one_c = sb("one_c", [P, 1])
        ones = sb("ones", [P, P])
        ident = sb("ident", [P, P])
        ssum = sb("ssum", [P, TOK])
        lnm = sb("lnm", [P, TOK])
        rstd = sb("rstd", [P, TOK])
        tmp = sb("tmp", [P, 2, TOK])
        lam_sb = rstd[:, :].rearrange("p (l a d) -> p l a d", l=2, a=4)
        lam_pr = lnm[:, 0:4 * DA_DIM].rearrange("p (l a d) -> p l a d", l=2, a=2)
        lam_sum = sb("lam_sum", [P, 2, 2])
        neg_lam = sb("neg_lam", [P, 2])
        subln = sb("subln", [P, 2])
        logit = sb("logit", [P, 2 * RET_HEADS])
        lg_t = sb("lg_t", [P, 4, 2 * RET_HEADS])
        log_g = sb("log_g", [P, 2, RET_HEADS])
        lg_cur = sb("lg_cur", [P, 2])

        with ExitStack() as s:
            u_hi = sb("u_hi", [P, JT, TOK], F32R, s)
            u_lo = sb("u_lo", [P, JT, TOK], F32R, s)
            ada_raw = sb("ada_raw", [P, ADA_RING, D], F32, s)
        with ExitStack() as s:
            sb("before_cond", [P, 2 * JT - 4, TOK], F32, s)
            cond_l = sb("cond_l", [P, 2, D], F32, s)
        with ExitStack() as s:
            ada_first = sb("ada_first", [P, 3 * ADA_GROUP, D], F32, s)
            sb("behind_values", [P, 4 * SEQ], F32, s)
            ada_rest = sb("ada_rest", [P, 2 * ADA_GROUP, D], F32, s)
            cond_0 = sb("cond_0", [P, 2, D], F32, s)
        with ExitStack() as s:
            y_hi = sb("y_hi", [P, KT, TOK], F32R, s)
            y_lo = sb("y_lo", [P, KT, TOK], F32R, s)
            v_all = sb("v_all", [P, 4, D], F32, s)
            da_rope = sb("da_rope", [P, 4, SEQ], F32, s)
            v_st = sb("v_st", [P, 4, P], F32, s)
            qT = sb("qT", [P, TOK], F32, s)
            kT = sb("kT", [P, TOK], F32, s)
            with ExitStack() as s2:
                qk_raw = sb("qk_raw", [P, 2, SEQ], F32, s2)
                rot = sb("rot", [P, 2, SEQ], F32, s2)
                e_x = sb("e_x", [P, 2, 2, TOK], F32, s2)
                e_z = sb("e_z", [P, 2, 2, CTX], F32, s2)
                a_x = sb("a_x", [P, 2, TOK], F32, s2)
                a_z = sb("a_z", [P, 2, CTX], F32, s2)
                aT = sb("aT", [P, 3, TOK], F32, s2)
                d_st = sb("d_st", [P, 4, 8], F32, s2)
            with ExitStack() as s2:
                rpb_rows = sb("rpb_rows", [NA_HEADS * 7, RPB_PAD], F32, s2)
                na_mask = sb("na_mask", [P, GRID_W], F32, s2)
                bias = sb("bias", [P, 2, 2, 2, SEQ], F32, s2)
                n_x = sb("n_x", [P, 2, 2, TOK], F32, s2)
                n_z = sb("n_z", [P, 2, 2, CTX], F32, s2)
                nT = sb("nT", [P, 2, 3, TOK], F32, s2)
                n_st = sb("n_st", [P, 3, 8], F32, s2)
        with ExitStack() as s:
            ry_hi = sb("ry_hi", [P, RET_HEADS * ET, TOK], F32R, s)
            ry_lo = sb("ry_lo", [P, RET_HEADS * ET, TOK], F32R, s)
            rv = sb("rv", [P, 4, RET_V], F32, s)
            rq = sb("rq", [P, 4, TOK], F32, s)
            ret_rope = sb("ret_rope", [P, 2, SEQ], F32, s)
            ret_exp = sb("ret_exp", [P, 4, 2, SEQ], F16, s)
            decay = sb("decay", [P, 2, 2, SEQ], F32, s)
            darg = sb("darg", [P, 2, SEQ], F32, s)
            sT = sb("sT", [P, 3, TOK], F32, s)
        rpb_skew = nc.dram_tensor("rpb_skew", (NA_HEADS * 7, GRID_W, RPB_PAD), F32, kind="Internal").ap()

        bank = [ctx.enter_context(nc.psum_tensor(f"bank{b}", [P, TOK], F32)) for b in range(8)]

        raw_loaded = [sem(f"raw_loaded{r}") for r in range(RING)]
        small_in, x_loaded, table_in = sem("small_in"), sem("x_loaded"), sem("table_in")
        hi_ready, lo_ready, unit_used = sem("hi_ready"), sem("lo_ready"), sem("unit_used")
        ada_loaded = [sem(f"ada_loaded{r}") for r in range(ADA_RING)]
        first_loaded = [sem(f"first_loaded{g}") for g in range(ADA_FIRST // ADA_GROUP)]
        cond_loaded = sem("cond_loaded")
        rest_loaded = [sem(f"rest_loaded{g}") for g in range(2)]
        ada_done, mod_ready, cond_ready, consts = sem("ada_done"), sem("mod_ready"), sem("cond_ready"), sem("consts")
        dve_own, act_own = sem("dve_own"), sem("act_own")
        lam_sums, lam_exps, log_abs, log_parts = sem("lam_sums"), sem("lam_exps"), sem("log_abs"), sem("log_parts")
        x_new, sq_ready, ssum_step = sem("x_new"), sem("sq_ready"), sem("ssum_step")
        ms_done, rstd_ready = sem("ms_done"), sem("rstd_ready")
        norm_t, h_hi_ready, h_ready = sem("norm_t"), sem("h_hi_ready"), sem("h_ready")
        fin_ready, stored = sem("fin_ready"), sem("stored")
        skew_in, skew_out, rpb_zero = sem("skew_in"), sem("skew_out"), sem("rpb_zero")
        bias_in = [sem("bias_in0"), sem("bias_in1")]

        plan = []
        first_unit = 0
        for li in range(layers):
            plan.append(Layer(sem, li, first_unit))
            first_unit += MIXER_UNITS[KINDS[li]] + FFN_UNITS
        UN = first_unit
        SMALL = 16 * 7
        LOOPED = 6
        NORMS = 2 * layers

        block = ctx.enter_context(nc.Block())

        def gate_buf(e):
            return lnm[:, :] if e % 2 == 0 else darg[:, :, :].rearrange("p a n -> p (a n)")

        @block.sync
        def _(sp):
            def loads(c, i=0, stride=0):
                if c >= UN:
                    return
                r = c % RING
                if c >= RING:
                    sp.wait_ge(lo_ready, i * stride + (c - RING + 1))
                sp.dma_start(w_raw[:, r, :], weights[bass.ds(i * stride + c, 1)]
                             .rearrange("a p n -> (a p) n")).then_inc(raw_loaded[r], 16)

            def load_range(c, end):
                end = min(end, UN)
                while (end - c) % RING:
                    loads(c)
                    c += 1
                if end > c:
                    with sp.Fori(0, (end - c) // RING) as i:
                        for j in range(RING):
                            loads(c + j, i, RING)

            def ada_group(a, dst):
                return sp.dma_start(dst, ada_w[a:a + ADA_GROUP].rearrange("a p n -> p a n"))

            def ada_first_load(g):
                at = ADA_GROUP * (g % 3)
                ada_group(g * ADA_GROUP, ada_first[:, at:at + ADA_GROUP, :]).then_inc(first_loaded[g], 16)

            def ada_rest_load(g):
                if g >= 2:
                    sp.wait_ge(ada_done, ADA_FIRST + ADA_GROUP * (g - 1))
                at = ADA_GROUP * (g % 2)
                ada_group(ADA_FIRST + g * ADA_GROUP, ada_rest[:, at:at + ADA_GROUP, :]).then_inc(rest_loaded[g % 2], 16)

            def ada_load(la, r, i):
                sp.wait_ge(ada_done, i * LOOPED + (r + MOD * la - 1))
                sp.dma_start(ada_raw[:, r % 2, :], ada_w[bass.ds(i * LOOPED + (r + MOD * la), 1)]
                             .rearrange("a p n -> (a p) n")).then_inc(ada_loaded[r % 2], 16)

            sp.dma_start(cond_0[:, :, :], cond_in.partition_broadcast(P)).then_inc(cond_loaded, 16)
            for dst, src in ((bias_ada, ada_b), (gain, gains), (gain_f, final_g), (subln, subln_in),
                             (ident, ident_in)):
                sp.dma_start(dst[tuple([slice(None)] * len(dst.shape))], src).then_inc(small_in, 16)
            sp.dma_start(lam_sb[:, :, :, :], lam_in.partition_broadcast(P)).then_inc(small_in, 16)
            sp.dma_start(logit[:, :], decay_in.partition_broadcast(P)).then_inc(small_in, 16)
            ada_first_load(0)
            sp.dma_start(xT[:, :, :], xT_in).then_inc(x_loaded, 16)
            ada_first_load(1)
            ada_first_load(2)
            sp.wait_ge(ada_done, ADA_GROUP)
            ada_first_load(3)
            loads(0)
            loads(1)
            ada_rest_load(0)
            loads(2)
            loads(3)
            ada_rest_load(1)
            at = RING
            for g in range(2, 6):
                loads(at)
                loads(at + 1)
                at += 2
                ada_rest_load(g)
            ada_rest_load(6)
            ada_rest_load(7)
            for L in plan:
                if L.li + 1 < layers:
                    load_range(at, L.nf + RING)
                    sp.wait_ge(rstd_ready, 2 * L.li + 2)
                    sp.dma_start(cond_l[:, :, :], cond_in.partition_broadcast(P)).then_inc(cond_loaded, 16)
                    with sp.Fori(0, MOD // LOOPED) as i:
                        for j, group in enumerate(((0,), (1, 2), (3,), (4, 5))):
                            loads(L.nf + RING + j, i, RING)
                            for r in group:
                                ada_load(L.li + 1, r, i)
                    at = L.nf + RING * (MOD // LOOPED + 1)
            load_range(at, UN)
            sp.wait_ge(fin_ready, KT)
            sp.dma_start(out, xT[:, :, 0:SEQ if layers == DEPTH else TOK]).then_inc(stored, 16)
            sp.wait_ge(stored, 16)

        @block.gpsimd
        def _(pool):
            nc.gpsimd.memset(ones[:, :], 1.0).then_inc(consts, 1)
            nc.gpsimd.memset(eps_c[:, :], EPS).then_inc(consts, 1)
            nc.gpsimd.memset(one_c[:, :], 1.0).then_inc(consts, 1)
            with pool.Fori(0, UN // RING) as i:
                for r in range(RING):
                    pool.wait_ge(hi_ready, i * RING + r + 1)
                    nc.gpsimd.tensor_tensor(out=w_lo[:, r, :], in0=w_raw[:, r, :], in1=w_hi[:, r, :],
                                            op=ALU.subtract).then_inc(lo_ready, 1)

        @block.tensor
        def _(pe):
            def mm(dst, lhsT, rhs, start, stop, **kw):
                return nc.tensor.matmul(dst, lhsT, rhs, start=start, stop=stop, **kw)

            def three(dst, stat, mov, start, stop, **kw):
                mm(dst, stat[0], mov[0], start, False, **kw)
                mm(dst, stat[0], mov[1], False, False, **kw)
                return mm(dst, stat[1], mov[0], False, stop, **kw)

            def weight(slot, a, b):
                r = slot % RING
                return w_hi[:, r, a:b], w_lo[:, r, a:b]

            def take(n):
                pe.wait_ge(lo_ready, n + 1)

            def unit(n, slot, dst, src, W, k0=0, start=True, stop=True, tiles=range(KT)):
                take(n)
                for k in tiles:
                    last = three(dst[:, 0:W], weight(slot, k * P, k * P + P),
                                 (src[0][:, k0 + k, 0:W], src[1][:, k0 + k, 0:W]),
                                 start and k == 0, stop and k == KT - 1)
                return last

            H = (h_hi, h_lo)

            def unit_pair(n, slot, banks, W, q):
                take(n + 1)
                for k in range(KT):
                    pe.wait_ge(h_ready, q * KT + k + 1)
                    for g in range(2):
                        last = three(banks[g][:, 0:W], weight(slot + g, k * P, k * P + P),
                                     (h_hi[:, k, 0:W], h_lo[:, k, 0:W]), k == 0, k == KT - 1)
                last.then_inc(unit_used, 2)

            def norm(q, W):
                pe.wait_ge(ssum_step, KT * (q + 1))
                mm(bank[7][:, 0:W], ones[:, :], ssum[:, 0:W], True, True).then_inc(ms_done, 1)

            def values(L, q):
                with pe.Fori(0, 2) as i:
                    for s in range(4):
                        take(i * 4 + (L.n + s))
                        for kk in range(2):
                            k = 2 * s + kk
                            pe.wait_ge(h_ready, q * KT + k + 1)
                            for tb in range(4):
                                last = three(bank[tb][:, :], tuple(t[:, k, tb * P:tb * P + P] for t in H),
                                             weight(L.n + s, kk * 512, kk * 512 + 512), k == 0, k == KT - 1)
                                if k == KT - 1 and tb < 3:
                                    last.then_inc(L.v_done, 1)
                        last.then_inc(unit_used, 1)
                    pe.wait_ge(L.v_act, i * 2 + 2)
                    pe.wait_ge(L.v_dve, i * 2 + 2)

            def attention(L):
                n = L.n + KT
                subs = 2 if L.na else 1
                per = L.groups // subs

                def transposes(t, sub):
                    for g in range(per):
                        if sub == 1:
                            pe.wait_ge(L.aT_ready, t * L.groups + (g + 1))
                        for c in range(4):
                            kb, qb = (c // 2, c % 2) if g == 0 else (g + 1, c) if L.zq else (2 + c // 2, c % 2)
                            src = n_x[:, qb % 2, sub, :] if L.na else a_x[:, qb % 2, :]
                            if qb >= 2:
                                src = n_z[:, sub, qb - 2, :] if L.na else a_z[:, qb - 2, :]
                                kb -= 2
                            last = nc.tensor.transpose(bank[g][:, c * P:c * P + P], src[:, kb * P:kb * P + P],
                                                       ident[:, :])
                        last.then_inc(L.t_done, 1)

                def values_product(t, sub):
                    pe.wait_ge(L.aT_ready, t * L.groups + per * (sub + 1))
                    lo, hi = (64 * sub, 64 * sub + 64) if L.na else (0, P)
                    for j, kb in enumerate((2, 3, 0, 1)):
                        if kb >= 2 and L.zq:
                            g, a, w = kb - 1, 0, TOK
                        else:
                            g, a, w = kb // 2, (kb % 2) * SEQ, SEQ
                        mov = (nT[:, sub, g, a:a + w] if L.na else aT[:, g, a:a + w])
                        last = mm(bank[6][lo:hi, 0:w], v_st[:, kb, lo:hi], mov, j == 0, j == 3)
                    return last

                def back(t):
                    pe.wait_ge(L.a_ready, t + 1)
                    for sub in range(subs):
                        transposes(t, sub)
                    pe.wait_ge(L.vst_ready, t + 1)
                    for sub in range(subs):
                        last = values_product(t, sub)
                    last.then_inc(L.pv_done, 1)

                def mean_square(t):
                    pe.wait_ge(L.osq_ready, t + 1)
                    mm(bank[7][:, 0:L.W], ones[:, :], tmp[:, 1, 0:L.W], True, True).then_inc(L.oms_done, 1)

                def score(j):
                    lo, hi = 64 * (j % 2), 64 * (j % 2) + 64
                    if j < 4:
                        qb = j // 2
                        last = mm(bank[j][:, :], qT[lo:hi, qb * P:qb * P + P], kT[lo:hi, :], True, True)
                    else:
                        for qb in range(2):
                            last = mm(bank[j][:, qb * CTX:qb * CTX + CTX],
                                      qT[lo:hi, SEQ + qb * P:SEQ + qb * P + P], kT[lo:hi, SEQ:TOK], True, True)
                    last.then_inc(L.s_done, 1)

                def tile(t, slot, place):
                    if place >= 2:
                        pe.wait_ge(L.y_lo_ready if L.na else L.y_ready, t - 1)
                    unit(t * 2 + n, slot, bank[6], H, L.W).then_inc(unit_used, 1)
                    unit(t * 2 + (n + 1), slot + 1, bank[7], H, TOK).then_inc(unit_used, 1)
                    if place >= 1:
                        pe.wait_ge(L.qk_act, t * (1 if L.na else 2) + 1)
                        back(t - 1)
                    dv, ac = (1, 1) if L.na else (2, 2)
                    pe.wait_ge(L.qk_dve, t * dv + dv)
                    pe.wait_ge(L.qk_act, t * ac + ac)
                    for j in range(L.banks):
                        score(j)
                        if j == 1 and place >= 1 and not L.na:
                            mean_square(t - 1)

                tile(0, n, 0)
                tile(1, n + 2, 1)
                with pe.Fori(0, (KT - 2) // 2) as i:
                    for s in range(2):
                        tile(i * 2 + (2 + s), n + 2 * s, 2)
                pe.wait_ge(L.y_lo_ready if L.na else L.y_ready, KT - 1)
                back(KT - 1)
                return lambda: mean_square(KT - 1)

            def project(L, e0, last_mean_square):
                if L.kind != 1:
                    n = L.n + 3 * KT
                    pe.wait_ge(L.y_lo_ready, KT - 1)
                    for s in range(3):
                        unit(n + s, n + s, bank[s], (y_hi, y_lo), L.W, tiles=range(KT - 1), stop=False)
                        if s == 0 and not L.na:
                            last_mean_square()
                    pe.wait_ge(L.y_lo_ready, KT)
                    for s in range(3):
                        unit(n + s, n + s, bank[s], (y_hi, y_lo), L.W, tiles=(KT - 1,)).then_inc(unit_used, 1)
                    for s in range(3, KT):
                        if s >= 4:
                            pe.wait_ge(x_new, e0 + s - 3)
                        unit(n + s, n + s, bank[s % 4], (y_hi, y_lo), L.W).then_inc(unit_used, 1)
                else:
                    pe.wait_ge(L.y_ready, RET_HEADS * ET + 2)
                    n = L.n + 12 * RET_HEADS
                    with pe.Fori(0, 4) as i:
                        for s in range(2):
                            pe.wait_ge(x_new, i * 2 + (e0 + s - 1))
                            u = 2 * s
                            unit(i * 4 + (n + u), n + u, bank[s], (ry_hi, ry_lo), L.W, stop=False)\
                                .then_inc(unit_used, 1)
                            for k in range(KT):
                                pe.wait_ge(L.y_lo_ready, KT + k + 1)
                                last = unit(i * 4 + (n + u + 1), n + u + 1, bank[s], (ry_hi, ry_lo), L.W, KT,
                                            start=False, tiles=(k,))
                            last.then_inc(unit_used, 1)

            def retention(L, q):
                with pe.Fori(0, RET_HEADS) as h:
                    def head_unit(u, b, **kw):
                        unit(h * 12 + (L.n + u), L.n + u, bank[b], H, TOK, **kw).then_inc(unit_used, 1)

                    pe.wait_ge(L.ors_ready, h + 1)
                    pe.wait_ge(L.y_ready, h * ET + 2)
                    unit_pair(h * 12 + L.n, L.n, bank[0:2], TOK, q)
                    for u in range(2, 4):
                        pe.wait_ge(L.y_ready, h * ET + (u + 1))
                        head_unit(u, u)
                    for s in range(4):
                        take(h * 12 + (L.n + 4 + s))
                        for kk in range(2):
                            k = 2 * s + kk
                            for tb in range(4):
                                last = three(bank[4 + tb][:, :], tuple(t[:, k, tb * P:tb * P + P] for t in H),
                                             weight(L.n + s, kk * 512, kk * 512 + 512), k == 0, k == KT - 1)
                                if k == KT - 1 and tb < 3:
                                    last.then_inc(L.v_done, 1)
                        last.then_inc(unit_used, 1)
                    pe.wait_ge(L.rot_ready, h * 2 + 2)
                    pe.wait_ge(L.zcopy_ready, h * 4 + 4)
                    for kb in range(4):
                        dst, w = (bank[0][:, kb * SEQ:kb * SEQ + SEQ], SEQ) if kb < 2 else (bank[kb - 1][:, :], TOK)
                        for d in range(2):
                            last = mm(dst, rq[:, 2 + d, kb * P:kb * P + P], rq[:, d, 0:w], d == 0, d == 1)
                        if kb:
                            last.then_inc(L.s_done, 1)
                    head_unit(8, 3)
                    pe.wait_ge(L.sT_ready, h * 3 + 3)
                    head_unit(9, 0)
                    pe.wait_ge(L.v_act, h * 2 + 2)
                    pe.wait_ge(L.v_dve, h * 2 + 2)
                    for e in range(ET):
                        for j, kb in enumerate((2, 3, 0, 1)):
                            mov, w = (sT[:, 0, kb * SEQ:kb * SEQ + SEQ], SEQ) if kb < 2 else (sT[:, kb - 1, :], TOK)
                            last = mm(bank[4 + e][:, 0:w], rv[:, kb, e * P:e * P + P], mov, j == 0, j == 3)
                        last.then_inc(L.o_done, 1)
                    head_unit(10, 2)
                    for e in range(ET):
                        pe.wait_ge(L.osq_ready, h * ET + (e + 1))
                        mm(bank[1][:, :], ones[:, :], tmp[:, e % 2, :], e == 0, e == ET - 1).then_inc(L.oms_done, 1)
                    pe.wait_ge(L.y_ready, h * ET + (ET + 1))
                    head_unit(11, 3)

            def ffn(L, q):
                n, li = L.nf, L.li
                ada = li + 1 < layers
                with pe.Fori(0, JT // 2) as i:
                    for s in range(2):
                        pe.wait_ge(L.u_free, i * 2 + (s + 1))
                        if s == 0:
                            unit_pair(i * 4 + n, n, bank[0:2], L.W, q)
                        else:
                            for g in range(2, 4):
                                unit(i * 4 + (n + g), n + g, bank[g], H, L.W).then_inc(unit_used, 1)
                if ada:
                    pe.wait_ge(mod_ready, li + 3)
                n += 2 * JT
                lead = (JT // 2) % 4
                for half in range(2):
                    banks = bank[4:8] if half == 0 else bank[0:4]

                    def step(n_at, slot, k_at, first, signal):
                        take(n_at)
                        for kk in range(2):
                            pe.wait_ge(L.u_lo_ready, JT if half else k_at + (kk + 1))
                            mov = tuple(t[:, bass.ds(k_at + kk, 1), 0:L.W].rearrange("p a n -> p (a n)")
                                        for t in (u_hi, u_lo))
                            for m in range(4):
                                last = three(banks[m][:, 0:L.W],
                                             weight(slot, kk * 512 + m * P, kk * 512 + m * P + P),
                                             mov, first and kk == 0, True, skip_group_check=True)
                                if signal and kk == 1 and m < 3:
                                    last.then_inc(L.out_done, 1)
                        last.then_inc(unit_used, 1)

                    for s in range(lead):
                        step(n + s, n + s, 2 * s, s == 0, False)
                    with pe.Fori(0, JT // 8) as i:
                        for s in range(4):
                            step(i * 4 + (n + lead + s), n + lead + s, i * 8 + 2 * (lead + s), False, s == 3)
                    n += JT // 2

            pe.wait_ge(consts, 3)
            for L in plan:
                norm(2 * L.li, TOK)
                if L.kind == 1:
                    retention(L, 2 * L.li)
                    last_mean_square = None
                else:
                    values(L, 2 * L.li)
                    last_mean_square = attention(L)
                project(L, KT * (2 * L.li + 1), last_mean_square)
                norm(2 * L.li + 1, L.W)
                ffn(L, 2 * L.li + 1)
            norm(NORMS, plan[-1].W)

        @block.scalar
        def _(act):
            own = Links(act, act_own)

            def log_exp_tables():
                nc.scalar.preload_act_table_set("natural_log_exp_and_others")

            def conv(c, i=0, stride=0):
                if c >= UN:
                    return
                r = c % RING
                act.wait_ge(raw_loaded[r], i * (16 * stride // RING) + 16 * (c // RING + 1))
                if c >= RING:
                    act.wait_ge(unit_used, i * stride + (c - RING + 1))
                nc.scalar.activation(w_hi[:, r, :], w_raw[:, r, :], ACT.Copy).then_inc(hi_ready, 1)

            def convs(c, count):
                count = min(count, UN - c)
                lead = count % RING
                for j in range(lead):
                    conv(c + j)
                if count >= RING:
                    with act.Fori(0, count // RING) as i:
                        for j in range(RING):
                            conv(c + lead + j, i, RING)

            def square(e, m, W, slot):
                act.wait_ge(x_new, e)
                src = xT[:, m, 0:W] if isinstance(m, int) else xT[:, bass.ds(m, 1), 0:W].rearrange("p a n -> p (a n)")
                nc.scalar.activation(tmp[:, slot, 0:W], src, ACT.Square).then_inc(sq_ready, 1)

            def rsqrt(W, src, count, ready):
                own(nc.scalar.activation(lnm[:, 0:W], src, ACT.Ln, bias=eps_c[:, 0:1], scale=1.0 / count))
                nc.scalar.activation(rstd[:, 0:W], lnm[:, 0:W], ACT.Exp, scale=-0.5).then_inc(ready, 1)

            def norm(q, L, which, W):
                act.wait_ge(ms_done, q + 1)
                rsqrt(W, bank[7][:, 0:W], D, rstd_ready)
                if L is None:
                    return
                for m in range(KT):
                    act.wait_ge(norm_t, q * KT + m + 1)
                    for c in range(W // SEQ):
                        last = nc.scalar.activation(h_hi[:, m, c * SEQ:c * SEQ + SEQ],
                                                    tmp[:, m % 2, c * SEQ:c * SEQ + SEQ], ACT.Identity,
                                                    bias=mod[:, L.par, 3 * KT * which + m, c:c + 1])
                    last.then_inc(h_hi_ready, 1)

            def values(L):
                with act.Fori(0, 2) as i:
                    for s in range(3):
                        conv(L.n + AHEAD + s, i, 4)
                    for tb in (0, 2):
                        act.wait_ge(L.v_done, i * 3 + (tb + 1))
                        nc.scalar.activation(v_all[:, tb, bass.ds(i * 512, 512)], bank[tb][:, :], ACT.Copy)\
                            .then_inc(L.v_act, 1)
                    conv(L.n + AHEAD + 3, i, 4)

            def attention(L):
                n = L.n + KT

                def exps(t):
                    for j in range(L.banks):
                        sub = j % 2
                        st = n_st if L.na else d_st
                        act.wait_ge(L.negmax, t * L.banks + (j + 1))
                        if j < 4:
                            dst = (n_x if L.na else e_x)[:, j // 2, sub, :]
                            col = 4 * sub + j // 2
                            last = nc.scalar.activation(dst, bank[j][:, :], ACT.Exp, bias=st[:, 0, col:col + 1],
                                                        accum_out=st[:, 1, col:col + 1])
                        else:
                            for qb in range(2):
                                dst = (n_z if L.na else e_z)[:, sub, qb, :]
                                col = 4 * sub + 2 + qb
                                last = nc.scalar.activation(dst, bank[j][:, qb * CTX:qb * CTX + CTX], ACT.Exp,
                                                            bias=st[:, 0, col:col + 1],
                                                            accum_out=st[:, 1, col:col + 1])
                        last.then_inc(L.e_ready, 1)

                def finish(t, c=None, i=0):
                    act.wait_ge(L.v_dve, 4)
                    nc.scalar.activation(v_st[:, :, :], v_all[:, :, bass.ds(t * P, P)], ACT.Copy)\
                        .then_inc(L.vst_ready, 1)
                    per = L.groups // (2 if L.na else 1)
                    for g in range(L.groups):
                        act.wait_ge(L.t_done, t * L.groups + (g + 1))
                        dst = nT[:, g // per, g % per, :] if L.na else aT[:, g, :]
                        nc.scalar.activation(dst, bank[g % per][:, :], ACT.Copy).then_inc(L.aT_ready, 1)
                    if c is not None:
                        conv(c + AHEAD, i, 4)
                        conv(c + AHEAD + 1, i, 4)
                    act.wait_ge(L.pv_done, t + 1)
                    o = bank[6][:, 0:L.W]
                    y = y_hi[:, bass.ds(t, 1), 0:L.W].rearrange("p a n -> p (a n)")
                    if L.na:
                        nc.scalar.activation(y, o, ACT.Copy).then_inc(L.y_hi_ready, 1)
                    else:
                        nc.scalar.activation(tmp[:, 1, 0:L.W], o, ACT.Square).then_inc(L.osq_ready, 1)
                        act.wait_ge(L.oms_done, t + 1)
                        rsqrt(L.W, bank[7][:, 0:L.W], 2 * DA_DIM, L.ors_ready)
                        act.wait_ge(L.y_ready, t + 1)
                        nc.scalar.activation(y, tmp[:, 0, 0:L.W], ACT.Copy).then_inc(L.y_hi_ready, 1)

                def bias_load(t, slot):
                    row = GRID_W * RPB_PAD
                    for sub in range(2):
                        for qr in range(ROWS):
                            src = bass.AP(tensor=rpb_skew.tensor, offset=(ROWS - 1 - qr) * row + GRID_W - 1,
                                          ap=[[7 * row, NA_HEADS], [RPB_PAD - 1, GRID_W], [row, ROWS], [1, GRID_W]])
                            lo = GRID_W * (qr % 2)
                            dst = bias[lo:lo + GRID_W, slot, sub, qr // 2, :].rearrange("p (r k) -> p r k", k=GRID_W)
                            act.dma_start(dst, src[bass.ds(t * 2 + sub, 1)].rearrange("a c r k -> (a c) r k"))\
                               .then_inc(bias_in[slot], 16)

                def tile(t, c, i, place, slot):
                    if place:
                        exps(t - 1)
                    if L.na:
                        bias_load(t, slot)
                    if L.na:
                        act.wait_ge(unit_used, t * 2 + (n + 1))
                        nc.scalar.activation(qT[:, :], bank[6][:, :], ACT.Copy, scale=NA_DIM ** -0.5)\
                            .then_inc(L.qk_act, 1)
                    else:
                        if L.li == 0 and place == 0:
                            act.wait_ge(mod_ready, 2)
                        for x, (b, dst, scale) in enumerate(((bank[6], qT, DA_DIM ** -0.5), (bank[7], kT, 1.0))):
                            act.wait_ge(unit_used, t * 2 + (n + 1 + x))
                            last = nc.scalar.activation(qk_raw[:, x, :], b[:, 0:SEQ], ACT.Copy)
                            if x or L.zq:
                                last = nc.scalar.activation(dst[:, SEQ:TOK], b[:, SEQ:TOK], ACT.Copy, scale=scale)
                            last.then_inc(L.qk_act, 1)
                    if place:
                        finish(t - 1, c, i)
                    else:
                        conv(c + AHEAD)
                        conv(c + AHEAD + 1)

                tile(0, n, 0, False, 0)
                tile(1, n + 2, 0, True, 1)
                with own.loop((KT - 2) // 2, 0 if L.na else 2) as i:
                    for s in range(2):
                        tile(i * 2 + (2 + s), n + 4 + 2 * s, i, True, s)
                exps(KT - 1)
                finish(KT - 1)

            def project(L, e0):
                if L.kind != 1:
                    n = L.n + 3 * KT
                    for m in range(KT):
                        conv(n + AHEAD + m)
                        square(e0 + m + 1, m, L.W, m % 2)
                else:
                    n = L.n + 12 * RET_HEADS
                    with act.Fori(0, 4) as i:
                        for s in range(2):
                            conv(n + AHEAD + 2 * s, i, 4)
                            square(i * 2 + (e0 + s + 1), i * 2 + s, L.W, s)
                            conv(n + AHEAD + 2 * s + 1, i, 4)

            def retention(L):
                with own.loop(RET_HEADS, 1) as h:
                    def hconv(*us):
                        for u in us:
                            conv(L.n + AHEAD + u, h, 12)

                    act.wait_ge(L.darg_ready, h + 1)
                    nc.scalar.activation(decay[:, :, 1, :], darg[:, :, :], ACT.Exp)
                    nc.scalar.activation(decay[:, :, 0, :], ret_exp[:, 2, :, :], ACT.Exp, scale=lg_cur[:, 0:1])
                    nc.scalar.activation(lnm[:, :].rearrange("p (a n) -> p a n", a=2), ret_exp[:, 3, :, :], ACT.Exp,
                                         scale=lg_cur[:, 1:2]).then_inc(L.dexp_ready, 1)
                    for u in range(4):
                        act.wait_ge(unit_used, h * 12 + (L.n + u + 1))
                        nc.scalar.activation(rq[:, u, SEQ:TOK], bank[u][:, SEQ:TOK], ACT.Copy)\
                            .then_inc(L.zcopy_ready, 1)
                        hconv(u)
                    hconv(4, 5, 6)
                    for tb in (0, 2):
                        act.wait_ge(L.v_done, h * 3 + (tb + 1))
                        nc.scalar.activation(rv[:, tb, :], bank[4 + tb][:, :], ACT.Copy).then_inc(L.v_act, 1)
                    hconv(7, 8, 9)
                    for e in range(ET):
                        act.wait_ge(L.o_done, h * ET + (e + 1))
                        if e >= 2:
                            act.wait_ge(L.oms_done, h * ET + (e - 1))
                        nc.scalar.activation(tmp[:, e % 2, :], bank[4 + e][:, :], ACT.Square).then_inc(L.osq_ready, 1)
                    hconv(10)
                    act.wait_ge(L.oms_done, h * ET + ET)
                    rsqrt(TOK, bank[1][:, :], RET_V, L.ors_ready)

                    def gate(e):
                        if e == 0:
                            act.wait_ge(L.ors_ready, h + 2)
                        act.wait_ge(unit_used, h * 12 + (L.n + 9 + e))
                        nc.scalar.activation(gate_buf(e), bank[(3, 0, 2, 3)[e]][:, :], ACT.Silu).then_inc(L.silu_g, 1)

                    def high(e):
                        act.wait_ge(L.y_ready, h * ET + (ET + e + 1))
                        nc.scalar.activation(ry_hi[:, bass.ds(h * ET + e, 1), :].rearrange("p a n -> p (a n)"),
                                             tmp[:, e % 2, :], ACT.Copy).then_inc(L.y_hi_ready, 1)

                    gate(0)
                    gate(1)
                    high(0)
                    gate(2)
                    high(1)
                    gate(3)
                    high(2)
                    hconv(11)
                    high(3)
                    log_exp_tables()

            def ffn(L, e0):
                n, li = L.nf, L.li
                ada = li + 1 < layers
                if ada:
                    act.wait_ge(cond_loaded, 16 * (li + 2))
                    nc.scalar.activation(cond_l[:, :, :], cond_l[:, :, :], ACT.Silu).then_inc(cond_ready, 1)
                with act.Fori(0, JT // 2) as i:
                    for s in range(2):
                        act.wait_ge(unit_used, i * 4 + (n + 2 * s + 2))
                        nc.scalar.activation(lnm[:, 0:L.W], bank[2 * s][:, 0:L.W], ACT.Silu)\
                            .then_inc(L.silu_ready, 1)
                        conv(n + AHEAD + 2 * s, i, 4)
                        act.wait_ge(L.u_free, i * 2 + (s + 3))
                        nc.scalar.activation(u_hi[:, bass.ds(i * 2 + s, 1), 0:L.W].rearrange("p a n -> p (a n)"),
                                             tmp[:, s, 0:L.W], ACT.Copy).then_inc(L.u_hi_ready, 1)
                        conv(n + AHEAD + 2 * s + 1, i, 4)
                n += 2 * JT
                log_exp_tables()
                convs(n + AHEAD, JT // 2)
                for m in range(4):
                    square(e0 + m + 1, m, L.W, m % 2)
                convs(n + JT // 2 + AHEAD, JT // 2 - 1)
                square(e0 + 5, 4, L.W, 0)
                conv(n + JT + AHEAD - 1)
                for m in range(5, 8):
                    square(e0 + m + 1, m, L.W, m % 2)

            act.wait_ge(cond_loaded, 16)
            nc.scalar.activation(cond_0[:, :, :], cond_0[:, :, :], ACT.Silu).then_inc(cond_ready, 1)
            log_exp_tables()
            act.wait_ge(consts, 3)
            act.wait_ge(lam_sums, 1)
            nc.scalar.activation(lam_sum[:, :, :], lam_sum[:, :, :], ACT.Exp).then_inc(lam_exps, 1)
            act.wait_ge(log_abs, 1)
            own(nc.scalar.activation(lg_t[:, 1, :], lg_t[:, 0, :], ACT.Exp, scale=-1.0))
            nc.scalar.activation(lg_t[:, 2, :], lg_t[:, 1, :], ACT.Ln, bias=one_c[:, 0:1]).then_inc(log_parts, 1)
            act.wait_ge(x_loaded, 16)
            for m in range(KT):
                if m >= 2:
                    act.wait_ge(ssum_step, m - 1)
                square(KT, m, TOK, m % 2)
            for c in range(AHEAD):
                conv(c)
            for L in plan:
                norm(2 * L.li, L, 0, TOK)
                if L.kind == 0:
                    act.dma_start(da_rope[:, :, :], da_rope_in).then_inc(table_in, 16)
                    values(L)
                    attention(L)
                elif L.kind == 1:
                    act.dma_start(ret_rope[:, :, :], ret_rope_in).then_inc(table_in, 16)
                    act.dma_start(ret_exp[:, :, :, :], ret_exp_in).then_inc(table_in, 16)
                    retention(L)
                else:
                    act.dma_start(na_mask[:, :], na_mask_in).then_inc(table_in, 16)
                    act.wait_ge(rpb_zero, 1)
                    pad = GRID_W - NA_KW
                    act.dma_start(rpb_rows[:, pad:pad + RPB_W], rpb_in).then_inc(skew_in, 16)
                    act.wait_ge(skew_in, 16)
                    act.dma_start(rpb_skew, rpb_rows[:, :].unsqueeze(1).to_broadcast([7 * NA_HEADS, GRID_W, RPB_PAD]))\
                       .then_inc(skew_out, 16)
                    values(L)
                    act.wait_ge(skew_out, 16)
                    attention(L)
                project(L, KT * (2 * L.li + 1))
                norm(2 * L.li + 1, L, 1, L.W)
                ffn(L, KT * (2 * L.li + 2))
            norm(NORMS, None, 0, plan[-1].W)

        @block.vector
        def _(dve):
            own = Links(dve, dve_own)
            V = nc.vector

            def row(t, m, W):
                return t[:, m, 0:W] if isinstance(m, int) else t[:, bass.ds(m, 1), 0:W].rearrange("p a n -> p (a n)")

            def gate_of(L, which, m, c):
                at = m + KT * which
                if isinstance(m, int):
                    return mod[:, L.par, at, c:c + 1]
                return mod[:, L.par, bass.ds(at, 1), c:c + 1].rearrange("p a c -> p (a c)")

            def ada_product(r, w, cond):
                for c in range(2):
                    for half in range(2):
                        k = slice(half * 512, half * 512 + 512)
                        last = V.tensor_tensor_reduce(bank[4 + half][:, :], w[:, k], cond[:, c, k], 1.0, 0.0, ALU.mult,
                                                      ALU.add, accum_out=ada_sum[:, r, c, half:half + 1])
                    if c == 0:
                        own(last)
                last.then_inc(ada_done, 1)

            def ada_sums(par, a, count):
                own(V.tensor_tensor(out=mod[:, par, bass.ds(a, count), :].unsqueeze(3),
                                    in0=ada_sum[:, 0:count, :, 0:1], in1=ada_sum[:, 0:count, :, 1:2], op=ALU.add))

            def ada_first_group(g):
                dve.wait_ge(first_loaded[g], 16)
                for r in range(ADA_GROUP):
                    ada_product(r, ada_first[:, ADA_GROUP * (g % 3) + r, :], cond_0)
                    dve.wait_ge(ada_done, g * ADA_GROUP + r + 1)
                ada_sums(0, g * ADA_GROUP, ADA_GROUP)

            def ada_rest_groups(i):
                for g in range(2):
                    dve.wait_ge(rest_loaded[g], i * 16 + 16)
                    a = i * (2 * ADA_GROUP) + (ADA_FIRST + g * ADA_GROUP)
                    for r in range(ADA_GROUP):
                        ada_product(r, ada_rest[:, g * ADA_GROUP + r, :], cond_0)
                        dve.wait_ge(ada_done, a + (r + 1))
                    ada_sums(0, a, ADA_GROUP)

            def modulation(la, a0=0, a1=MOD):
                par = la % 2
                dve.wait_ge(ada_done, MOD * la + a1)
                own(V.tensor_tensor(out=mod[:, par, a0:a1, :], in0=mod[:, par, a0:a1, :],
                                    in1=bias_ada[:, la, a0:a1].unsqueeze(2).to_broadcast([P, a1 - a0, 2]), op=ALU.add))
                for j in range(a0 // ADA_FIRST, 1 + (a1 > ADA_FIRST)):
                    a = KT * (3 * j + 1)
                    last = V.scalar_tensor_tensor(out=amp[:, par, j, :, :], in0=mod[:, par, a:a + KT, :], scalar=1.0,
                                                  in1=gain[:, la, j, :].unsqueeze(2).to_broadcast([P, KT, 2]),
                                                  op0=ALU.add, op1=ALU.mult)
                last.then_inc(mod_ready, 1)
                dve.wait_ge(mod_ready, la + 1 + (a1 == MOD))

            def residual(L, which, src, m, W):
                for c in range(W // SEQ):
                    x = row_part(m, c)
                    last = V.scalar_tensor_tensor(out=x, in0=src[:, c * SEQ:c * SEQ + SEQ],
                                                  scalar=gate_of(L, which, m, c), in1=x, op0=ALU.mult, op1=ALU.add)
                last.then_inc(x_new, 1)

            def row_part(m, c):
                if isinstance(m, int):
                    return xT[:, m, c * SEQ:c * SEQ + SEQ]
                return xT[:, bass.ds(m, 1), c * SEQ:c * SEQ + SEQ].rearrange("p a n -> p (a n)")

            def add_square(e, slot, W, first=False):
                dve.wait_ge(sq_ready, e)
                if not first:
                    dve.wait_ge(ssum_step, e - 1)
                V.tensor_tensor(out=ssum[:, 0:W], in0=ssum[:, 0:W], in1=tmp[:, slot, 0:W], op=ALU.add)\
                    .then_inc(ssum_step, 1)

            def norm(q, L, which, W):
                dve.wait_ge(rstd_ready, q + 1)
                own(V.memset(ssum[:, :], 0.0))

                def scaled(m):
                    if m >= 2:
                        dve.wait_ge(h_ready, q * KT + m - 1)
                    for c in range(W // SEQ):
                        last = V.scalar_tensor_tensor(out=tmp[:, m % 2, c * SEQ:c * SEQ + SEQ],
                                                      in0=xT[:, m, c * SEQ:c * SEQ + SEQ],
                                                      scalar=amp[:, L.par, which, m, c:c + 1],
                                                      in1=rstd[:, c * SEQ:c * SEQ + SEQ], op0=ALU.mult, op1=ALU.mult)
                    last.then_inc(norm_t, 1)

                def low(m):
                    dve.wait_ge(h_hi_ready, q * KT + m + 1)
                    for c in range(W // SEQ):
                        s = slice(c * SEQ, c * SEQ + SEQ)
                        last = V.scalar_tensor_tensor(out=h_lo[:, m, s], in0=tmp[:, m % 2, s],
                                                      scalar=mod[:, L.par, 3 * KT * which + m, c:c + 1],
                                                      in1=h_hi[:, m, s].bitcast(F32), op0=ALU.add, op1=ALU.subtract)
                    last.then_inc(h_ready, 1)

                scaled(0)
                for m in range(1, KT):
                    scaled(m)
                    low(m - 1)
                low(KT - 1)

            def values(L):
                rounds, per = (MOD - ADA_FIRST) // (2 * ADA_GROUP), 2 * (ADA_GROUP + 1)
                with own.loop(2, per if L.li == 0 else 0) as i:
                    if L.li == 0:
                        ada_rest_groups(i)
                    for tb in (1, 3):
                        if tb == 1:
                            dve.wait_ge(L.v_done, i * 3 + 2)
                        else:
                            dve.wait_ge(unit_used, i * 4 + (L.n + 4))
                        V.tensor_copy(v_all[:, tb, bass.ds(i * 512, 512)], bank[tb][:, :]).then_inc(L.v_dve, 1)
                if L.li == 0:
                    for i in range(2, rounds):
                        ada_rest_groups(i)
                    modulation(0, ADA_FIRST, MOD)

            def rotate(src, dst, table):
                for quarter in range(4):
                    a, b = 32 * quarter, 32 * (quarter ^ 1)
                    V.tensor_tensor(out=rot[a:a + 32, 0, :], in0=src[b:b + 32, :],
                                    in1=da_rope[b:b + 32, table + 1, :], op=ALU.mult)
                own(V.tensor_tensor(out=rot[:, 1, :], in0=src, in1=da_rope[:, table, :], op=ALU.mult))
                return V.tensor_tensor(out=dst, in0=rot[:, 0, :], in1=rot[:, 1, :], op=ALU.add)

            def attention(L, e0):
                n = L.n + KT

                def weights_(t, slot):
                    st = n_st if L.na else d_st
                    if L.na:
                        dve.wait_ge(bias_in[slot], t * 64 + (128 - 64 * slot))
                        b = bias[:, slot, :, :, :].rearrange("p h q (r k) -> p (h q r) k", k=GRID_W)
                        own(V.tensor_tensor(out=b, in0=b,
                                            in1=na_mask[:, :].unsqueeze(1).to_broadcast([P, 4 * ROWS, GRID_W]),
                                            op=ALU.add))
                    for j in range(L.banks):
                        sub = j % 2
                        dve.wait_ge(L.s_done, t * L.banks + (j + 1))
                        if j < 4:
                            if L.na:
                                own(V.tensor_tensor(out=bank[j][:, 0:SEQ], in0=bank[j][:, 0:SEQ],
                                                    in1=bias[:, slot, sub, j // 2, :], op=ALU.add))
                            col = 4 * sub + j // 2
                            last = V.tensor_reduce(out=st[:, 0, col:col + 1], in_=bank[j][:, :], axis=AX.X, op=ALU.max,
                                                   negate=True)
                        else:
                            last = V.tensor_reduce(out=st[:, 0, 4 * sub + 2:4 * sub + 4],
                                                   in_=bank[j][:, :].rearrange("p (q k) -> p q k", q=2), axis=AX.X,
                                                   op=ALU.max, negate=True)
                        last.then_inc(L.negmax, 1)
                    dve.wait_ge(L.e_ready, t * L.banks + L.banks)
                    cols = 4 if L.zq else 2
                    grp = [st[:, k, :].rearrange("p (s c) -> p s c", s=2)[:, :, 0:cols] for k in range(3)]
                    own(V.reciprocal(grp[2], grp[1]))
                    if L.na:
                        for sub in range(2):
                            for qb in range(4):
                                x = n_x[:, qb, sub, :] if qb < 2 else n_z[:, sub, qb - 2, :]
                                last = V.tensor_scalar(x, x, st[:, 2, 4 * sub + qb:4 * sub + qb + 1], None, ALU.mult)
                    else:
                        own(V.tensor_scalar(st[:, 3, 0:cols], st[:, 2, 4:4 + cols], neg_lam[:, L.da:L.da + 1], None,
                                            ALU.mult))
                        parts = [(a_x[:, qb, :], e_x[:, qb, 0, :], e_x[:, qb, 1, :]) if qb < 2 else
                                 (a_z[:, qb - 2, :], e_z[:, 0, qb - 2, :], e_z[:, 1, qb - 2, :])
                                 for qb in range(cols)]
                        for qb, (a, x0, x1) in enumerate(parts):
                            ins = V.tensor_scalar(a, x0, st[:, 2, qb:qb + 1], None, ALU.mult)
                            if qb == cols - 1:
                                own(ins)
                        for qb, (a, x0, x1) in enumerate(parts):
                            last = V.scalar_tensor_tensor(out=a, in0=x1, scalar=st[:, 3, qb:qb + 1], in1=a,
                                                          op0=ALU.mult, op1=ALU.add)
                    last.then_inc(L.a_ready, 1)

                def finish(t):
                    if not L.na:
                        dve.wait_ge(L.ors_ready, t + 1)
                        V.scalar_tensor_tensor(out=tmp[:, 0, 0:L.W], in0=bank[6][:, 0:L.W],
                                               scalar=subln[:, L.da:L.da + 1], in1=rstd[:, 0:L.W], op0=ALU.mult,
                                               op1=ALU.mult).then_inc(L.y_ready, 1)
                    dve.wait_ge(L.y_hi_ready, t + 1)
                    V.tensor_tensor(out=row(y_lo, t, L.W), in0=bank[6][:, 0:L.W] if L.na else tmp[:, 0, 0:L.W],
                                    in1=row(y_hi, t, L.W), op=ALU.subtract).then_inc(L.y_lo_ready, 1)

                def tile(t, place, slot):
                    if place:
                        weights_(t - 1, 1 - slot)
                    if L.na:
                        dve.wait_ge(unit_used, t * 2 + (n + 2))
                        V.tensor_copy(kT[:, :], bank[7][:, :]).then_inc(L.qk_dve, 1)
                    else:
                        dve.wait_ge(L.qk_act, t * 2 + 1)
                        rotate(qk_raw[:, 0, :], qT[:, 0:SEQ], 0).then_inc(L.qk_dve, 1)
                        dve.wait_ge(L.qk_act, t * 2 + 2)
                        dve.wait_ge(L.qk_dve, t * 2 + 1)
                        rotate(qk_raw[:, 1, :], kT[:, 0:SEQ], 2).then_inc(L.qk_dve, 1)
                    if place:
                        finish(t - 1)

                tile(0, 0, 0)
                tile(1, 1, 1)
                per_tile = (1 + 4 + 1) if L.na else 3 + 2
                with own.loop((KT - 2) // 2, 2 * per_tile) as i:
                    for s in range(2):
                        tile(i * 2 + (2 + s), 1, s)
                weights_(KT - 1, 1)
                finish(KT - 1)

            def project(L, e0):
                per, body = (4, 4) if L.kind != 1 else (2, 2)
                n = L.n + (3 * KT if L.kind != 1 else 12 * RET_HEADS)
                with dve.Fori(0, KT // body) as i:
                    for s in range(body):
                        used = s + 1 if L.kind != 1 else 2 * s + 2
                        dve.wait_ge(unit_used, i * 4 + (n + used))
                        residual(L, 2, bank[s], i * body + s, L.W)
                        add_square(i * body + (e0 + s + 1), s % 2, L.W)

            def retention(L):
                with own.loop(RET_HEADS, 5 + ET) as h:
                    own(V.tensor_copy(lg_cur[:, :].unsqueeze(2), log_g[:, :, bass.ds(h, 1)]))
                    own(V.tensor_scalar(darg[:, :, :], ret_exp[:, 1, :, :], lg_cur[:, 1:2], None, ALU.mult))
                    V.scalar_tensor_tensor(out=darg[:, :, :], in0=ret_exp[:, 0, :, :], scalar=lg_cur[:, 0:1],
                                           in1=darg[:, :, :], op0=ALU.mult, op1=ALU.add).then_inc(L.darg_ready, 1)
                    dve.wait_ge(L.dexp_ready, h + 1)
                    own(V.tensor_tensor(out=decay[:, :, 0, :], in0=decay[:, :, 0, :],
                                        in1=lnm[:, :].rearrange("p (a n) -> p a n", a=2), op=ALU.add))
                    half = [tmp[:, j // 2, SEQ * (j % 2):SEQ * (j % 2) + SEQ] for j in range(4)]
                    for x in range(2):
                        dve.wait_ge(L.zcopy_ready, h * 4 + (2 * x + 2))
                        if x:
                            dve.wait_ge(L.rot_ready, h * 2 + 1)
                        for j, (b, tab) in enumerate(((0, 0), (1, 1), (0, 1), (1, 0))):
                            ins = V.tensor_tensor(out=half[j], in0=bank[2 * x + b][:, 0:SEQ], in1=ret_rope[:, tab, :],
                                                  op=ALU.mult)
                        own(ins)
                        V.tensor_tensor(out=rq[:, 2 * x, 0:SEQ], in0=half[0], in1=half[1], op=ALU.subtract)
                        V.tensor_tensor(out=rq[:, 2 * x + 1, 0:SEQ], in0=half[2], in1=half[3], op=ALU.add)\
                            .then_inc(L.rot_ready, 1)
                    for tb in (1, 3):
                        if tb == 1:
                            dve.wait_ge(L.v_done, h * 3 + 2)
                        else:
                            dve.wait_ge(unit_used, h * 12 + (L.n + 8))
                        V.tensor_copy(rv[:, tb, :], bank[4 + tb][:, :]).then_inc(L.v_dve, 1)
                    for g in range(3):
                        dve.wait_ge(L.s_done, h * 3 + (g + 1))
                        dec = decay[:, :, 1, :] if g == 0 else decay[:, g - 1, :, :]
                        V.scalar_tensor_tensor(out=sT[:, g, :].rearrange("p (a n) -> p a n", a=2),
                                               in0=bank[g][:, :].rearrange("p (a n) -> p a n", a=2),
                                               scalar=RET_QK ** -0.5, in1=dec, op0=ALU.mult, op1=ALU.mult)\
                            .then_inc(L.sT_ready, 1)

                    def gated(e):
                        dve.wait_ge(L.ors_ready, h + 2)
                        if e:
                            dve.wait_ge(L.y_ready, h * ET + (ET + e))
                        own(V.tensor_tensor(out=ssum[:, :], in0=bank[4 + e][:, :], in1=rstd[:, :], op=ALU.mult))
                        dve.wait_ge(L.silu_g, h * ET + (e + 1))
                        V.tensor_tensor(out=tmp[:, e % 2, :], in0=ssum[:, :], in1=gate_buf(e), op=ALU.mult)\
                            .then_inc(L.y_ready, 1)

                    def low(e):
                        dve.wait_ge(L.y_hi_ready, h * ET + (e + 1))
                        V.tensor_tensor(out=row(ry_lo, h * ET + e, TOK), in0=tmp[:, e % 2, :],
                                        in1=row(ry_hi, h * ET + e, TOK), op=ALU.subtract).then_inc(L.y_lo_ready, 1)

                    gated(0)
                    for e in range(1, ET):
                        gated(e)
                        low(e - 1)
                    low(ET - 1)
                own(V.memset(ssum[:, :], 0.0))

            def ffn(L, e0):
                n, li = L.nf, L.li
                ada = li + 1 < layers
                dve.sem_inc(L.u_free, 2)
                if ada:
                    dve.wait_ge(cond_ready, li + 2)

                def hidden(i):
                    for s in range(2):
                        dve.wait_ge(L.silu_ready, i * 2 + (s + 1))
                        V.tensor_tensor(out=tmp[:, s, 0:L.W], in0=bank[2 * s + 1][:, 0:L.W], in1=lnm[:, 0:L.W],
                                        op=ALU.mult).then_inc(L.u_free, 1)
                        some = LOOPED // 2 if ada and not late else 0

                        def ada_unit(r):
                            dve.wait_ge(ada_loaded[r % 2], i * (8 * LOOPED) + 16 * (li * (MOD // 2) + r // 2 + 1))
                            ada_product(r % some, ada_raw[:, r % 2, :], cond_l)
                            dve.wait_ge(ada_done, i * LOOPED + (r + 1 + MOD * (li + 1)))

                        if some:
                            ada_unit(s * some)
                        dve.wait_ge(L.u_hi_ready, i * 2 + (s + 1))
                        V.tensor_tensor(out=row(u_lo, i * 2 + s, L.W), in0=tmp[:, s, 0:L.W],
                                        in1=row(u_hi, i * 2 + s, L.W), op=ALU.subtract).then_inc(L.u_lo_ready, 1)
                        if some:
                            for r in range(s * some + 1, (s + 1) * some):
                                ada_unit(r)
                            ada_sums((li + 1) % 2, i * LOOPED + s * some, some)

                late = False
                first = MOD // LOOPED
                if ada:
                    with own.loop(first, LOOPED + 2) as i:
                        hidden(i)
                    modulation(li + 1)
                    late = True
                    with dve.Fori(first, JT // 2) as i:
                        hidden(i)
                else:
                    with dve.Fori(0, JT // 2) as i:
                        hidden(i)
                n += 2 * JT
                for half in range(2):
                    banks = bank[4:8] if half == 0 else bank[0:4]
                    n += JT // 2
                    for m in range(4):
                        if m < 3:
                            dve.wait_ge(L.out_done, 6 * half + 3 + m + 1)
                        else:
                            dve.wait_ge(unit_used, n)
                        residual(L, 5, banks[m], 4 * half + m, L.W)
                        if m:
                            add_square(e0 + 4 * half + m, (m - 1) % 2, L.W)
                    add_square(e0 + 4 * half + 4, 1, L.W)

            dve.sem_inc(x_new, KT)
            for L in plan:
                if L.kind == 1:
                    dve.sem_inc(L.y_ready, ET)
                    dve.sem_inc(L.ors_ready, 1)
            own(V.memset(ssum[:, :], 0.0))
            dve.wait_ge(small_in, SMALL)
            pairs = lam_sb[:, :, :, :].rearrange("p l (a b) d -> p l a b d", b=2)
            own(V.tensor_tensor(out=lam_pr[:, :, :, :], in0=pairs[:, :, :, 0, :], in1=pairs[:, :, :, 1, :], op=ALU.mult))
            V.tensor_reduce(out=lam_sum[:, :, :], in_=lam_pr[:, :, :, :], axis=AX.X, op=ALU.add).then_inc(lam_sums, 1)
            V.scalar_tensor_tensor(out=lg_t[:, 0, :], in0=logit[:, :], scalar=-1.0, in1=logit[:, :], op0=ALU.mult,
                                   op1=ALU.max).then_inc(log_abs, 1)
            own(V.tensor_scalar(lg_t[:, 3, :], logit[:, :], 0.0, None, ALU.min))
            dve.wait_ge(lam_exps, 1)
            own(V.tensor_tensor(out=neg_lam[:, :].unsqueeze(2), in0=lam_sum[:, :, 1:2], in1=lam_sum[:, :, 0:1],
                                op=ALU.subtract))
            da_layers = [li for li in range(DEPTH) if KINDS[li] == 0]
            for j, li in enumerate(da_layers):
                init = 0.8 - 0.6 * math.exp(-0.3 * li)
                V.tensor_scalar(neg_lam[:, j:j + 1], neg_lam[:, j:j + 1], -init, None, ALU.add)
                own(V.tensor_scalar(subln[:, j:j + 1], subln[:, j:j + 1], 1.0 - init, None, ALU.mult))
            dve.wait_ge(log_parts, 1)
            own(V.tensor_tensor(out=log_g[:, :, :], in0=lg_t[:, 3, :].rearrange("p (a h) -> p a h", a=2),
                                in1=lg_t[:, 2, :].rearrange("p (a h) -> p a h", a=2), op=ALU.subtract))
            dve.wait_ge(cond_ready, 1)
            ada_first_group(0)
            for m in range(KT):
                add_square(m + 1, m % 2, TOK, first=m == 0)
            for g in range(1, ADA_FIRST // ADA_GROUP):
                ada_first_group(g)
            modulation(0, 0, ADA_FIRST)
            tables = 0
            for L in plan:
                if L.kind == 2:
                    dve.wait_ge(rstd_ready, 2 * L.li + 1)
                    V.memset(rpb_rows[:, :], 0.0).then_inc(rpb_zero, 1)
                norm(2 * L.li, L, 0, TOK)
                tables += 2 if L.kind == 1 else 1
                dve.wait_ge(table_in, 16 * tables)
                if L.kind == 1:
                    retention(L)
                else:
                    values(L)
                    attention(L, 0)
                project(L, KT * (2 * L.li + 1))
                norm(2 * L.li + 1, L, 1, L.W)
                ffn(L, KT * (2 * L.li + 2))
            dve.wait_ge(rstd_ready, NORMS + 1)
            for m in range(KT):
                if layers == DEPTH:
                    V.scalar_tensor_tensor(out=xT[:, m, 0:SEQ], in0=xT[:, m, 0:SEQ], scalar=gain_f[:, m:m + 1],
                                           in1=rstd[:, 0:SEQ], op0=ALU.mult, op1=ALU.mult).then_inc(fin_ready, 1)
                else:
                    dve.sem_inc(fin_ready, 1)


def _tall(w, c):
    k = w.shape[0] // P
    u = w[:, c:c + P].reshape(k // KT, KT, P, P)
    return list(u.transpose(0, 2, 1, 3).reshape(k // KT, P, KT * P))


def _wide(w, c):
    u = w[:, c:c + 512].reshape(w.shape[0] // (2 * P), 2, P, 512)
    return list(u.transpose(0, 2, 1, 3).reshape(-1, P, 1024))


def _stream(inputs, layers):
    units = []
    seen = {0: 0, 1: 0, 2: 0}
    for li in range(layers):
        kind = KINDS[li]
        at = seen[kind]
        seen[kind] += 1
        if kind == 1:
            w, wo = inputs["ret_w_in"][at], inputs["ret_w_o"][at]
            for h in range(RET_HEADS):
                for c in (h * 2 * P, h * 2 * P + P, D + h * 2 * P, D + h * 2 * P + P):
                    units += _tall(w, c)
                units += _wide(w, 2 * D + h * RET_V)
                for e in range(ET):
                    units += _tall(w, 4 * D + h * RET_V + e * P)
        else:
            w, wo = (inputs["da_w_qkv"][at], inputs["da_w_o"][at]) if kind == 0 else                 (inputs["na_w_qkv"][at], inputs["na_w_o"][at])
            units += _wide(w, 2 * D) + _wide(w, 2 * D + 512)
            for t in range(KT):
                units += _tall(w, t * P) + _tall(w, D + t * P)
        for m in range(KT):
            units += _tall(wo, m * P)
        w = inputs["ffn_in"][li]
        for j in range(JT):
            units += _tall(w, j * P) + _tall(w, HIDDEN + j * P)
        units += _wide(inputs["ffn_out"][li], 0) + _wide(inputs["ffn_out"][li], 512)
    return np.stack(units)


def kernel(layers=DEPTH, **inputs):
    import concourse.bacc as _bacc
    from concourse.bass_utils import run_bass_kernel_spmd as _run

    a = {k: np.asarray(v) for k, v in inputs.items()}
    arrays = {
        "xT": np.concatenate([a["x"][0], a["ctx"][0]], 0).T.reshape(KT, P, TOK).transpose(1, 0, 2),
        "cond": np.stack([a["c"][0], a["c_ctx"]]),
        "weights": _stream(a, layers),
        "ada_w": a["w_ada"].transpose(0, 2, 1).reshape(DEPTH * MOD, P, D),
        "ada_b": a["b_ada"].reshape(DEPTH, MOD, P).transpose(2, 0, 1),
        "gains": a["norm_g"].reshape(DEPTH, 2, KT, P).transpose(3, 0, 1, 2),
        "final_g": a["final_g"].reshape(KT, P).T,
        "lam": a["da_lambda"],
        "subln": a["da_subln"].T,
        "decay": a["ret_decay"][0].reshape(-1),
        "rpb": a["na_rpb"][0][:, NA_KH - ROWS:NA_KH + ROWS - 1, :].reshape(NA_HEADS * 7, RPB_W),
        **shape_tables(),
    }
    arrays = {f"in_{k}": np.ascontiguousarray(v) for k, v in arrays.items()}
    nc = _bacc.Bacc("TRN2", target_bir_lowering=False, num_devices=1)
    args = [nc.dram_tensor(k, v.shape, mybir.dt.from_np(v.dtype), kind="ExternalInput").ap()
            for k, v in arrays.items()]
    W = SEQ if layers == DEPTH else TOK
    out = nc.dram_tensor("out_x", (P, KT, W), F32, kind="ExternalOutput").ap()
    trunk(nc, *args, out, layers=layers)
    r = _run(nc, [arrays], core_ids=[0])
    got = r.results[0]["out_x"]
    return got.transpose(1, 0, 2).reshape(D, W).T.reshape(1, W, D)
```
